# Optimizing a Trainium2 kernel written in Bass

```python
import math
import jax, jax.numpy as jnp
from jax import lax
import numpy as np

D_MODEL = 1024
BATCH = 1
SEQ = 1024
DEPTH = 1

EPS = 1e-6
GLA_HEADS = 4
GLA_DK = 48
GLA_DV = 96
GLA_GATE_RANK = 16
GLA_GATE_NORM = 16.0
GLA_CHUNK = 64
DSA_HEADS = 6
DSA_DH = 64
IDX_HEADS = 4
IDX_DIM = 32
TOPK_MAX = 256
QUERY_BLOCK = 128
POOL_GROUPS = 4
POOL_GC = 64
POOL_WINDOWS = (2, 4, 8, 16)
REL_BUCKETS = 32
REL_MAX_DIST = 128

GLA_W = GLA_HEADS * GLA_DV
DSA_W = DSA_HEADS * DSA_DH
POOL_W = POOL_GROUPS * POOL_GC
D_MIX = GLA_W + DSA_W + POOL_W

IN_SIZES = (
    GLA_HEADS * GLA_DK,
    GLA_HEADS * GLA_DK,
    GLA_W,
    GLA_GATE_RANK,
    GLA_W,
    DSA_W,
    DSA_W,
    DSA_W,
    DSA_W,
    IDX_HEADS * IDX_DIM,
    IDX_DIM,
    IDX_HEADS,
    POOL_W,
    POOL_W,
)
IN_COLS = sum(IN_SIZES)


def split_cols(p):
    outs = []
    off = 0
    for s in IN_SIZES:
        outs.append(p[..., off:off + s])
        off += s
    return outs

def rmsnorm(x, g):
    xf = x.astype(jnp.float32)
    y = xf * lax.rsqrt(jnp.mean(xf * xf, axis=-1, keepdims=True) + EPS)
    return (y * g.astype(jnp.float32)).astype(x.dtype)

def t5_bucket(rel):
    rel = jnp.maximum(rel, 0)
    max_exact = REL_BUCKETS // 2
    relf = jnp.maximum(rel, 1).astype(jnp.float32)
    large = max_exact + (jnp.log(relf / max_exact) / math.log(REL_MAX_DIST / max_exact)
                         * (REL_BUCKETS - max_exact)).astype(jnp.int32)
    large = jnp.minimum(large, REL_BUCKETS - 1)
    return jnp.where(rel < max_exact, rel, large)

def gla_mixer(q, k, v, glog):
    B, T, H, dk = q.shape
    dv = v.shape[-1]
    N = T // GLA_CHUNK
    def chunk(a):
        return a.astype(jnp.float32).reshape(B, N, GLA_CHUNK, H, a.shape[-1])
    qf, kf, vf, gf = chunk(q), chunk(k), chunk(v), chunk(glog)
    b = jnp.cumsum(gf, axis=2)
    b_last = b[:, :, -1:]
    qe = qf * jnp.exp(b) * (dk ** -0.5)
    ke = kf * jnp.exp(-b)
    kd = kf * jnp.exp(b_last - b)
    A = jnp.einsum('bnihd,bnjhd->bnhij', qe, ke)
    tril = jnp.tril(jnp.ones((GLA_CHUNK, GLA_CHUNK), dtype=bool))
    A = jnp.where(tril, A, 0.0)
    o_intra = jnp.einsum('bnhij,bnjhv->bnihv', A, vf)
    U = jnp.einsum('bnjhd,bnjhv->bnhdv', kd, vf)
    decay = jnp.exp(b_last[:, :, 0])
    def step(S, inp):
        dec, u = inp
        return dec[..., None] * S + u, S
    S0 = jnp.zeros((B, H, dk, dv), jnp.float32)
    _, S_prev = lax.scan(step, S0, (jnp.moveaxis(decay, 1, 0), jnp.moveaxis(U, 1, 0)))
    S_prev = jnp.moveaxis(S_prev, 0, 1)
    o_inter = jnp.einsum('bnihd,bnhdv->bnihv', qe, S_prev)
    return (o_intra + o_inter).reshape(B, T, H, dv)

def dsa_mixer(q, k, v, q_idx, k_idx, w_idx, rel_bias):
    B, T, H, dh = q.shape
    topk = min(TOPK_MAX, T // 4)
    NB = T // QUERY_BLOCK
    def blk(a):
        return jnp.moveaxis(a.reshape(B, NB, QUERY_BLOCK, *a.shape[2:]), 1, 0)
    pos_blk = jnp.arange(T, dtype=jnp.int32).reshape(NB, QUERY_BLOCK)
    key_pos = jnp.arange(T, dtype=jnp.int32)
    kidx_f = k_idx.astype(jnp.float32)
    rb = rel_bias.astype(jnp.float32)

    def body(args):
        qb, qib, wb, tq = args
        s = jax.nn.relu(jnp.einsum('bqhd,bsd->bqhs', qib.astype(jnp.float32), kidx_f)
                        * (IDX_DIM ** -0.5))
        score = jnp.einsum('bqhs,bqh->bqs', s, wb.astype(jnp.float32) * (IDX_HEADS ** -0.5))
        visible = key_pos[None, :] <= tq[:, None]
        score = jnp.where(visible[None], score, -jnp.inf)
        _, idx = lax.top_k(score, topk)
        kg = jax.vmap(lambda kk, ii: kk[ii])(k, idx)
        vg = jax.vmap(lambda vv, ii: vv[ii])(v, idx)
        logits = jnp.einsum('bqhd,bqkhd->bhqk', qb.astype(jnp.float32),
                            kg.astype(jnp.float32)) * (dh ** -0.5)
        rel = tq[None, :, None] - idx
        bias = rb[t5_bucket(rel)]
        logits = logits + jnp.moveaxis(bias, -1, 1)
        logits = jnp.where((rel >= 0)[:, None], logits, -1e30)
        p = jax.nn.softmax(logits, axis=-1)
        o = jnp.einsum('bhqk,bqkhd->bqhd', p, vg.astype(jnp.float32))
        return o.astype(q.dtype)

    o = lax.map(body, (blk(q), blk(q_idx), blk(w_idx), pos_blk))
    return jnp.moveaxis(o, 0, 1).reshape(B, T, H * dh)

def pool_mixer(u, pool_w, pool_scale):
    B, T, _ = u.shape
    ug = u.astype(jnp.float32).reshape(B, T, POOL_GROUPS, POOL_GC)
    cs = jnp.cumsum(ug, axis=1)
    pos = jnp.arange(T, dtype=jnp.int32)
    outs = []
    for gi, w in enumerate(POOL_WINDOWS):
        c = cs[:, :, gi]
        lower = jnp.pad(c, ((0, 0), (w, 0), (0, 0)))[:, :T]
        cnt = jnp.minimum(pos + 1, w).astype(jnp.float32)[None, :, None]
        outs.append((c - lower) / cnt - ug[:, :, gi])
    pooled = jnp.stack(outs, axis=2)
    y = jnp.einsum('btgc,gcd->btgd', pooled, pool_w.astype(jnp.float32)).reshape(B, T, POOL_W)
    return (y * pool_scale.astype(jnp.float32)).astype(u.dtype)

def first_inputs(seed: int = 0) -> dict:
    key = jax.random.key(seed)
    ks = jax.random.split(key, 12)
    f = jnp.float32
    x = jax.random.normal(ks[0], (BATCH, SEQ, D_MODEL), f)
    norm_g = 1.0 + 0.05 * jax.random.normal(ks[1], (DEPTH, D_MODEL), f)
    w_in = jax.random.normal(ks[2], (DEPTH, D_MODEL, IN_COLS), f) * D_MODEL ** -0.5
    gla_gate_w2 = jax.random.normal(ks[3], (DEPTH, GLA_GATE_RANK, GLA_HEADS * GLA_DK), f) * GLA_GATE_RANK ** -0.5
    gla_gate_b = 0.1 * jax.random.normal(ks[4], (DEPTH, GLA_HEADS * GLA_DK), f)
    gla_norm_g = 1.0 + 0.05 * jax.random.normal(ks[5], (DEPTH, GLA_DV), f)
    rel_bias = 0.1 * jax.random.normal(ks[6], (REL_BUCKETS, DSA_HEADS), f)
    pool_w = jax.random.normal(ks[7], (DEPTH, POOL_GROUPS, POOL_GC, POOL_GC), f) * POOL_GC ** -0.5
    pool_scale = 1.0 + 0.1 * jax.random.normal(ks[8], (DEPTH, POOL_W), f)
    w_out = jax.random.normal(ks[9], (DEPTH, D_MIX, D_MODEL), f) * D_MIX ** -0.5
    final_norm_g = 1.0 + 0.05 * jax.random.normal(ks[10], (D_MODEL,), f)
    return {'x': x, 'norm_g': norm_g, 'w_in': w_in, 'gla_gate_w2': gla_gate_w2,
            'gla_gate_b': gla_gate_b, 'gla_norm_g': gla_norm_g, 'rel_bias': rel_bias,
            'pool_w': pool_w, 'pool_scale': pool_scale, 'w_out': w_out,
            'final_norm_g': final_norm_g}

def first_block(x, norm_g, w_in, gla_gate_w2, gla_gate_b, gla_norm_g, rel_bias,
              pool_w, pool_scale, w_out, final_norm_g):
    B, T, _ = x.shape
    for l in range(DEPTH):
        h = rmsnorm(x, norm_g[l])
        p = jnp.einsum('btd,dc->btc', h, w_in[l])
        (gq, gk, gv, gz, ggate, dq, dk, dv, dgate,
         qi, ki, wi, pu, pgate) = split_cols(p)
        glog = jax.nn.log_sigmoid((jnp.einsum('btr,rc->btc', gz, gla_gate_w2[l])
                                   + gla_gate_b[l]).astype(jnp.float32)) / GLA_GATE_NORM
        o_gla = gla_mixer(gq.reshape(B, T, GLA_HEADS, GLA_DK),
                          gk.reshape(B, T, GLA_HEADS, GLA_DK),
                          gv.reshape(B, T, GLA_HEADS, GLA_DV),
                          glog.reshape(B, T, GLA_HEADS, GLA_DK))
        o_gla = rmsnorm(o_gla, gla_norm_g[l]).reshape(B, T, GLA_W).astype(x.dtype)
        y_gla = o_gla * jax.nn.silu(ggate)
        o_dsa = dsa_mixer(dq.reshape(B, T, DSA_HEADS, DSA_DH),
                          dk.reshape(B, T, DSA_HEADS, DSA_DH),
                          dv.reshape(B, T, DSA_HEADS, DSA_DH),
                          qi.reshape(B, T, IDX_HEADS, IDX_DIM), ki, wi, rel_bias)
        y_dsa = o_dsa * jax.nn.silu(dgate)
        y_pool = pool_mixer(pu, pool_w[l], pool_scale[l]) * jax.nn.silu(pgate)
        y = jnp.concatenate([y_gla, y_dsa, y_pool], axis=-1)
        x = x + jnp.einsum('btc,cd->btd', y, w_out[l])
    return rmsnorm(x, final_norm_g)


DEPTH_2 = 2

PLE_DIM = 256
N_MIXERS = 2
N_FOX_LAYERS = (DEPTH_2 + 1) // 2
N_DIL_LAYERS = DEPTH_2 // 2

FOX_HEADS = 16
FOX_HEAD_DIM = D_MODEL // FOX_HEADS
FOX_WIDTH = FOX_HEADS * FOX_HEAD_DIM
FOX_IN = 4 * FOX_WIDTH + FOX_HEADS
FORGET_BIAS_CENTER = 2.0

DIL_PATTERN = ((128, 1), (512, 4), (2048, 16))
DIL_GROUPS = len(DIL_PATTERN)
DIL_HEADS_PER_GROUP = 8
DIL_HEAD_DIM = D_MODEL // DIL_HEADS_PER_GROUP
DIL_HEADS = DIL_GROUPS * DIL_HEADS_PER_GROUP
DIL_QKV = DIL_HEADS * DIL_HEAD_DIM
DIL_WIDTH = DIL_HEADS_PER_GROUP * DIL_HEAD_DIM
DIL_IN = 3 * DIL_QKV + DIL_WIDTH
ALIBI_MAX_EXP = 8.0

RMS_EPS = 1e-6


def rms_norm(x, g):
    xf = x.astype(jnp.float32)
    y = xf * lax.rsqrt(jnp.mean(xf * xf, axis=-1, keepdims=True) + RMS_EPS)
    return (y * g.astype(jnp.float32)).astype(x.dtype)

def alibi_slopes(n):
    return 2.0 ** (-ALIBI_MAX_EXP * jnp.arange(1, n + 1, dtype=jnp.float32) / n)

def fox_mixer(h, w_in, b_f, w_out):
    B, S, _ = h.shape
    proj = h @ w_in
    q = proj[..., :FOX_WIDTH].reshape(B, S, FOX_HEADS, FOX_HEAD_DIM)
    k = proj[..., FOX_WIDTH:2 * FOX_WIDTH].reshape(B, S, FOX_HEADS, FOX_HEAD_DIM)
    v = proj[..., 2 * FOX_WIDTH:3 * FOX_WIDTH].reshape(B, S, FOX_HEADS, FOX_HEAD_DIM)
    z = proj[..., 3 * FOX_WIDTH:4 * FOX_WIDTH]
    f_logit = proj[..., 4 * FOX_WIDTH:]
    log_f = jax.nn.log_sigmoid((f_logit + b_f).astype(jnp.float32))
    c = jnp.cumsum(log_f, axis=1)
    nb = S // QUERY_BLOCK
    qb = q.reshape(B, nb, QUERY_BLOCK, FOX_HEADS, FOX_HEAD_DIM).transpose(1, 0, 2, 3, 4)
    cqb = c.reshape(B, nb, QUERY_BLOCK, FOX_HEADS).transpose(1, 0, 3, 2)
    qpos = jnp.arange(S).reshape(nb, QUERY_BLOCK)
    kpos = jnp.arange(S)
    ck = c.transpose(0, 2, 1)
    scale = FOX_HEAD_DIM ** -0.5

    def block(args):
        qi, ci, pi = args
        s = jnp.einsum('bqhd,bkhd->bhqk', qi, k).astype(jnp.float32) * scale
        s = s + ci[..., None] - ck[:, :, None, :]
        s = jnp.where((kpos[None, :] <= pi[:, None])[None, None], s, -jnp.inf)
        pr = jax.nn.softmax(s, axis=-1)
        return jnp.einsum('bhqk,bkhd->bqhd', pr.astype(v.dtype), v)

    o = lax.map(block, (qb, cqb, qpos))
    o = o.transpose(1, 0, 2, 3, 4).reshape(B, S, FOX_WIDTH)
    return (o * jax.nn.silu(z)) @ w_out

def dilated_window_attention(q, k, v, slopes, window, dilation):
    B, S, Hg, hd = q.shape
    L = S // dilation
    nW = window // dilation
    nb = -(-L // nW)
    Lp = nb * nW
    Bd = B * dilation

    def to_blocks(t):
        t = t.reshape(B, L, dilation, Hg, hd).transpose(0, 2, 1, 3, 4).reshape(Bd, L, Hg, hd)
        t = jnp.pad(t, ((0, 0), (0, Lp - L), (0, 0), (0, 0)))
        return t.reshape(Bd, nb, nW, Hg, hd)

    def with_prev(t):
        prev = jnp.pad(t, ((0, 0), (1, 0), (0, 0), (0, 0), (0, 0)))[:, :-1]
        return jnp.concatenate([prev, t], axis=2)

    qb = to_blocks(q)
    kk = with_prev(to_blocks(k))
    vv = with_prev(to_blocks(v))
    i = jnp.arange(nW)[:, None]
    j = jnp.arange(2 * nW)[None, :]
    dist = nW + i - j
    key_pos = (jnp.arange(nb)[:, None, None] - 1) * nW + j[None]
    valid = (dist >= 0)[None] & (dist <= nW)[None] & (key_pos >= 0)
    bias = -slopes.astype(jnp.float32)[:, None, None] * (dist * dilation).astype(jnp.float32)
    scale = hd ** -0.5
    s = jnp.einsum('znqhd,znkhd->znhqk', qb, kk).astype(jnp.float32) * scale + bias[None, None]
    s = jnp.where(valid[None, :, None], s, -jnp.inf)
    lse = jax.nn.logsumexp(s, axis=-1, keepdims=True)
    pr = jnp.exp(s - lse)
    o = jnp.einsum('znhqk,znkhd->znqhd', pr.astype(v.dtype), vv)
    o = o.reshape(Bd, Lp, Hg, hd)[:, :L]
    o = o.reshape(B, dilation, L, Hg, hd).transpose(0, 2, 1, 3, 4).reshape(B, S, Hg, hd)
    lse = lse[..., 0].transpose(0, 1, 3, 2).reshape(Bd, Lp, Hg)[:, :L]
    lse = lse.reshape(B, dilation, L, Hg).transpose(0, 2, 1, 3).reshape(B, S, Hg)
    return o, lse

def dilated_mixer(h, w_in, w_out):
    B, S, _ = h.shape
    proj = h @ w_in
    shp = (B, S, DIL_GROUPS, DIL_HEADS_PER_GROUP, DIL_HEAD_DIM)
    q = proj[..., :DIL_QKV].reshape(shp)
    k = proj[..., DIL_QKV:2 * DIL_QKV].reshape(shp)
    v = proj[..., 2 * DIL_QKV:3 * DIL_QKV].reshape(shp)
    z = proj[..., 3 * DIL_QKV:]
    slopes = alibi_slopes(DIL_HEADS).reshape(DIL_GROUPS, DIL_HEADS_PER_GROUP)
    outs, lses = [], []
    for g, (window, dilation) in enumerate(DIL_PATTERN):
        o, l = dilated_window_attention(q[:, :, g], k[:, :, g], v[:, :, g], slopes[g], window, dilation)
        outs.append(o)
        lses.append(l)
    wts = jax.nn.softmax(jnp.stack(lses), axis=0)
    o = jnp.sum(wts[..., None] * jnp.stack(outs).astype(jnp.float32), axis=0)
    o = o.astype(h.dtype).reshape(B, S, DIL_WIDTH)
    return (o * jax.nn.silu(z)) @ w_out

def second_inputs(seed: int = 0) -> dict:
    key = jax.random.key(seed)
    ks = jax.random.split(key, 14)
    f32 = jnp.float32
    nrm = lambda k, shape, fan_in: jax.random.normal(k, shape, f32) * fan_in ** -0.5
    return {
        "x": jax.random.normal(ks[0], (BATCH, SEQ, D_MODEL), f32),
        "p": jax.random.normal(ks[1], (DEPTH_2, BATCH, SEQ, PLE_DIM), f32),
        "fox_norm": 1.0 + 0.02 * jax.random.normal(ks[2], (N_FOX_LAYERS, D_MODEL), f32),
        "fox_w_in": nrm(ks[3], (N_FOX_LAYERS, D_MODEL, FOX_IN), D_MODEL),
        "fox_b_f": FORGET_BIAS_CENTER + 0.5 * jax.random.normal(ks[4], (N_FOX_LAYERS, FOX_HEADS), f32),
        "fox_w_out": nrm(ks[5], (N_FOX_LAYERS, FOX_WIDTH, D_MODEL), FOX_WIDTH),
        "dil_norm": 1.0 + 0.02 * jax.random.normal(ks[6], (N_DIL_LAYERS, D_MODEL), f32),
        "dil_w_in": nrm(ks[7], (N_DIL_LAYERS, D_MODEL, DIL_IN), D_MODEL),
        "dil_w_out": nrm(ks[8], (N_DIL_LAYERS, DIL_WIDTH, D_MODEL), DIL_WIDTH),
        "ple_w_up": nrm(ks[9], (DEPTH_2, PLE_DIM, D_MODEL), PLE_DIM),
        "ple_w_gate": nrm(ks[10], (DEPTH_2, D_MODEL, D_MODEL), D_MODEL),
        "final_norm": 1.0 + 0.02 * jax.random.normal(ks[11], (D_MODEL,), f32),
    }

def second_block(x, p, fox_norm, fox_w_in, fox_b_f, fox_w_out, dil_norm, dil_w_in, dil_w_out,
              ple_w_up, ple_w_gate, final_norm):
    h = x
    for i in range(DEPTH_2):
        j = i // N_MIXERS
        if i % N_MIXERS == 0:
            h = h + fox_mixer(rms_norm(h, fox_norm[j]), fox_w_in[j], fox_b_f[j], fox_w_out[j])
        else:
            h = h + dilated_mixer(rms_norm(h, dil_norm[j]), dil_w_in[j], dil_w_out[j])
        h = h + (p[i] @ ple_w_up[i]) * jax.nn.sigmoid(h @ ple_w_gate[i])
    return rms_norm(h, final_norm)


def setup_inputs(seed=0):
    out = dict(first_inputs(seed))
    for name, value in second_inputs(seed + 1).items():
        if name != "x":
            out[name + "_2"] = value
    return out


def reference(
    x, norm_g, w_in, gla_gate_w2, gla_gate_b, gla_norm_g, rel_bias, pool_w, pool_scale, w_out,
    final_norm_g, p_2, fox_norm_2, fox_w_in_2, fox_b_f_2, fox_w_out_2, dil_norm_2, dil_w_in_2,
    dil_w_out_2, ple_w_up_2, ple_w_gate_2, final_norm_2,
):
    x = first_block(
        x, norm_g, w_in, gla_gate_w2, gla_gate_b, gla_norm_g, rel_bias, pool_w, pool_scale,
        w_out, final_norm_g,
    )
    return second_block(
        x, p_2, fox_norm_2, fox_w_in_2, fox_b_f_2, fox_w_out_2, dil_norm_2, dil_w_in_2,
        dil_w_out_2, ple_w_up_2, ple_w_gate_2, final_norm_2,
    )


_drawn_inputs = setup_inputs


def setup_inputs(seed=0):
    import zlib

    import numpy as np

    out = dict(_drawn_inputs(seed))
    spreads = {}
    factors = {'gla_gate_b': 4.31,
     'gla_norm_g': 3.595,
     'rel_bias': 8.0,
     'pool_scale': 2.77,
     'fox_norm_2': 8.0,
     'dil_norm_2': 8.0}
    for name, (base, spread) in spreads.items():
        noise = np.random.default_rng([zlib.crc32(name.encode()), seed]).standard_normal(out[name].shape)
        drawn = base * np.exp(spread * noise) if base else spread * noise
        out[name] = __import__('jax').numpy.asarray(drawn.astype(out[name].dtype))
    for name, factor in factors.items():
        out[name] = (out[name] * factor).astype(out[name].dtype)
    return out
```

```python
from contextlib import ExitStack
import math

import numpy as np
import concourse.bass as bass
from concourse import mybir

F32 = mybir.dt.float32
F32R = mybir.dt.float32r
BF16 = mybir.dt.bfloat16
I32 = mybir.dt.int32
ALU = mybir.AluOpType
ACT = mybir.ActivationFunctionType
AX = mybir.AxisListType

P = 128
T = 1024
D = 1024
KB = D // P
NT = T // P
EPS = 1e-6
NEG = -1e30

GH, DK, DV, CH = 4, 48, 96, 64
SIZES = (GH * DK, GH * DK, GH * DV, 16, GH * DV, 384, 384, 384, 384, 128, 32, 4, 256, 256)
OFF = [sum(SIZES[:n]) for n in range(len(SIZES))]
(C_GQ, C_GK, C_GV, C_GZ, C_GG, C_DQ, C_DK, C_DV, C_DG, C_QI, C_KI, C_WI, C_PU, C_PG) = OFF
TOPK = 256
IDX_H, IDX_D = 4, 32
DIL_PATTERN = ((128, 1), (512, 4), (2048, 16))
DIL_NB = [min(w // P + 1, NT) for w, _ in DIL_PATTERN]

N_FIRST = 18
W_DSA = N_FIRST
W_OUT1 = W_DSA + 3 * 4
W_FOXF = W_OUT1 + 8
W_FOX = W_FOXF + 1
W_OUT2 = W_FOX + 8 * 4
W_PLE0 = W_OUT2 + 8
W_DIL = W_PLE0 + 10
W_OUT3 = W_DIL + 8 * 10
W_PLE1 = W_OUT3 + 8
W_ALL = W_PLE1 + 10
PLE_EXTRA = 6


def attention_steps(kind):
    steps = []
    if kind == "dil":
        for i in range(NT):
            segs, col = [], 0
            for g, buf, c0 in ((2, 0, 0), (0, 1, 0), (1, 1, 256)):
                nb = min(DIL_NB[g], i + 1)
                segs.append((g, buf, c0, i + 1 - nb, nb, col))
                col += nb * P
            steps.append((i, 0, segs, col))
    else:
        for s in range(2 * NT):
            i = s // 2
            steps.append((i, s % 2, [(0, s % 2, 0, 0, i + 1, 0)], (i + 1) * P))
    return steps


def chunks_of(steps):
    out = []
    for _, _, _, width in steps:
        n = width // P
        out.append([(b, min(4, n - b)) for b in range(0, n, 4)])
    if sum(map(len, out)) % 2:
        out[0] = [(b, min(2, 3 - b)) for b in range(0, 3, 2)]
    return out


def chunk_starts(chunks):
    starts = [0]
    for c in chunks:
        starts.append(starts[-1] + len(c))
    assert starts[-1] % 2 == 0
    return starts


def value_cols(head):
    at, lo, out = head * DV, 0, []
    while lo < DV:
        w = min(DV - lo, P - (at + lo) % P)
        out.append((lo, (at + lo) // P, (at + lo) % P, w))
        lo += w
    return out


def mask_offset(i):
    return P * (i * (i + 1) // 2)


def host_constants():
    q = np.arange(P)[:, None]
    out = {}
    out["c_ident"] = np.eye(P, dtype=np.float32)
    out["c_flip"] = np.eye(P, dtype=np.float32)[::-1].copy()
    out["c_ones"] = np.ones((P, P), np.float32)
    out["c_diag"] = np.where(q >= np.arange(P)[None, :], 0.0, NEG).astype(np.float32)
    cols = []
    for (window, dil), nb in zip(DIL_PATTERN, DIL_NB):
        dist = q + (nb - 1) * P - np.arange(nb * P)[None, :]
        ok = (dist >= 0) & (dist <= window) & (dist % dil == 0)
        cols.append(np.where(ok, dist, 1e30).astype(np.float32))
    out["c_dist"] = np.concatenate(cols, axis=1)
    out["c_slope"] = np.broadcast_to(-(2.0 ** (-8.0 * np.arange(1, 25) / 24.0)), (P, 24)).astype(np.float32).copy()
    rel = np.maximum(255 - np.arange(384), 0)
    relf = np.maximum(rel, 1).astype(np.float32)
    large = 16 + (np.log(relf / np.float32(16)) / np.float32(math.log(8.0)) * np.float32(16)).astype(np.int32)
    bucket = np.where(rel < 16, rel, np.minimum(large, 31))
    out["c_bucket"] = (np.arange(32)[:, None] == bucket[None, :]).astype(np.float32)
    j = np.arange(P)[:, None]
    i = np.arange(P)[None, :]
    out["c_chunk"] = ((j // CH == i // CH) & (j <= i)).astype(np.int32)
    out["c_keep"] = np.broadcast_to((np.arange(T) % CH != 0), (P, T)).astype(np.float32).copy()
    cnt = np.zeros((2, P, T), np.float32)
    for g, w in enumerate((2, 4, 8, 16)):
        cnt[g // 2, (g % 2) * 64:(g % 2) * 64 + 64, :] = 1.0 / np.minimum(np.arange(T) + 1, w)
    out["c_cnt"] = cnt
    return out


def build(nc, a, stop=99):
    ctx = ExitStack()
    with ctx:
        def sb(name, shape, dt=F32):
            return ctx.enter_context(nc.sbuf_tensor(name, shape, dt))

        def ps(name, shape):
            return ctx.enter_context(nc.psum_tensor(name, shape, F32))

        def sem(name):
            return ctx.enter_context(nc.semaphore(name))

        hT = sb("hT", [P, KB, T])
        act_hi = sb("act_hi", [P, KB, T], F32R)
        act_lo = sb("act_lo", [P, KB, T], F32R)
        w_raw = sb("w_raw", [P, 2, KB, P])
        w_hi = sb("w_hi", [P, 2, KB, P], F32R)
        w_lo = sb("w_lo", [P, 2, KB, P], F32R)
        ident = sb("ident", [P, P])
        ones = sb("ones", [P, P])
        diag = sb("diag", [P, P])
        gains = sb("gains", [P, 5, KB])
        epsc = sb("epsc", [P, 1])
        A_COLS = 21900
        arena = sb("arena", [P, A_COLS])

        proj = [ps("proj0", [P, 512]), ps("proj1", [P, 512])]
        score = ps("score", [P, 2, 1024])
        obanks = [ps("out0", [P, 512]), ps("out1", [P, 512])]
        obank = obanks[0]

        yd = nc.dram_tensor("y_scratch", [D, T], F32).ap()
        xd = nc.dram_tensor("x_scratch", [P, KB, T], F32).ap()
        cd = nc.dram_tensor("decay_scratch", [16, T], F32).ap()
        rd = nc.dram_tensor("bias_scratch", [6, 384], F32).ap()

        class Area:
            def __init__(self, tensor, at=0, end=A_COLS):
                self.t, self.at, self.end = tensor, at, end

            def take(self, n):
                r = self.t[:, self.at:self.at + n]
                self.at += n
                assert self.at <= self.end, (self.at, self.end)
                return r

        w_loaded = [sem("w_loaded0"), sem("w_loaded1")]
        w_hi_done = sem("w_hi_done")
        w_split = sem("w_split")
        pass_done = [sem("pass_done0"), sem("pass_done1")]
        pass_free = [sem("pass_free0"), sem("pass_free1")]
        consts = sem("consts")
        eps_set = sem("eps_set")
        phase_end = sem("phase_end")

        def wait(eng, s, v):
            if isinstance(v, int) and v <= 0:
                return
            eng.wait_ge(s, v)

        def wait_turn(eng, s, it, per, local):
            if local > 0:
                eng.wait_ge(s, it * per + local)

        def barrier(eng, k):
            eng.drain().then_inc(phase_end, 1)
            eng.wait_ge(phase_end, 3 * k)

        def wview(ap):
            return ap.rearrange("(k p) c -> p k c", p=P)

        w_in = wview(a["w_in"][0])
        w_out = [wview(a["w_out"][0]), wview(a["fox_w_out_2"][0]), wview(a["dil_w_out_2"][0])]
        w_fox = wview(a["fox_w_in_2"][0])
        w_dil = wview(a["dil_w_in_2"][0])
        w_gate = [wview(a["ple_w_gate_2"][m]) for m in range(2)]
        w_up = [wview(a["ple_w_up_2"][m]) for m in range(2)]
        NCONST = 3 + 5

        h_flat = hT[:, :, :].rearrange("p k t -> p (k t)")
        F = Area(h_flat, 0, KB * T)
        gq = F.take(2 * T).rearrange("p (g t) -> p g t", g=2)
        gk = F.take(2 * T).rearrange("p (g t) -> p g t", g=2)
        gv = F.take(3 * T).rearrange("p (b t c) -> p b t c", b=3, c=P)
        amask = F.take(P).bitcast(I32)
        intra = F.take(4 * P).rearrange("p (n c) -> p n c", n=4)
        G = Area(arena)
        maskb = G.take(mask_offset(NT) // 2).bitcast(BF16)
        tbias = G.take(6 * 256).rearrange("p (h c) -> p h c", h=6)
        rb31 = G.take(6)
        wi_s = G.take(4 * NT).rearrange("p (t h) -> p t h", h=4)
        gw2 = G.take(2 * P).rearrange("p (g c) -> p g c", g=2)
        gb = G.take(2)
        gnorm = G.take(DV)
        pscale = G.take(2)
        pw = G.take(2 * P).rearrange("p (g c) -> p g c", g=2)
        state = G.take(2 * 192).rearrange("p (g c) -> p g c", g=2)
        gzT = G.take(T)
        gg = G.take(3 * T).rearrange("p (b t) -> p b t", b=3)
        pu = G.take(2 * T).rearrange("p (b t) -> p b t", b=2)
        pg = G.take(2 * T).rearrange("p (b t) -> p b t", b=2)
        at_tmp = G.at
        qiT, kiT = G.take(T), G.take(T)
        rel_s = G.take(2 * T).rearrange("p (n t) -> p n t", n=2)
        work = G.take(T)
        top8 = G.take(8)
        G2 = Area(arena, at_tmp)
        gb_x = G2.take(2 * T).rearrange("p (g t) -> p g t", g=2)
        gb_e = G2.take(2 * T).rearrange("p (g t) -> p g t", g=2)
        g_o = G2.take(3 * T).rearrange("p (t c) -> p t c", c=GH * DV)
        kdN = G2.take(2 * P).rearrange("p (n c) -> p n c", n=2)
        g_ms = G2.take(2 * GH * NT)
        dec = G2.take(2 * NT * 2).rearrange("p (g c) -> p g c", g=2)
        G3 = Area(arena, at_tmp)
        pa, pb = (G3.take(2 * T).rearrange("p (b t) -> p b t", b=2) for _ in range(2))
        pcnt = G3.take(2 * T).rearrange("p (b t) -> p b t", b=2)

        def attention_area(area, groups, width):
            r = {}
            r["q"] = [area.take(T) for _ in range(groups)]
            r["k"] = [area.take(T) for _ in range(groups)]
            r["v"] = [area.take(T).rearrange("p (t c) -> p t c", c=P) for _ in range(groups)]
            r["g"] = area.take(T)
            r["e"] = area.take(T)
            r["p"] = [area.take(width) for _ in range(2)]
            r["pT"] = area.take(1024).rearrange("p (n c) -> p n c", n=2)
            r["o"] = area.take(256).rearrange("p (n c) -> p n c", n=2)
            r["y"] = area.take(T)
            r["st"] = area.take(3 * 16)
            return r

        fields = dict(
            dsa=attention_area(Area(arena, mask_offset(NT) // 2 + 6 * 256 + 6), 1, T),
        )
        FX = Area(arena)
        fields["fox"] = attention_area(FX, 1, T)
        cB = [FX.take(T) for _ in range(2)]
        ccol = FX.take(16 * NT).rearrange("p (t h) -> p t h", h=16)
        crow = FX.take(T)
        ctmp = FX.take(T)
        fb = FX.take(1)
        DL = Area(arena)
        fields["dil"] = attention_area(DL, 3, sum(DIL_NB) * P)
        cdist = DL.take(sum(DIL_NB) * P)
        cslope = DL.take(24)
        N = Area(arena)
        nsq = [N.take(T) for _ in range(2)]
        nacc = N.take(T)
        ntmp = [N.take(T) for _ in range(2)]
        Y = Area(arena)
        yin = Y.take(KB * T).rearrange("p (k t) -> p k t", k=KB)
        xnat = Y.take(2 * T).rearrange("p (n c) -> p n c", n=2)
        U = Area(arena)
        upT = U.take(KB * T).rearrange("p (k t) -> p k t", k=KB)
        pnat = U.take(NT * 256).rearrange("p (t c) -> p t c", c=256)
        ple_e = [U.take(512) for _ in range(2)]
        ple_t = [U.take(512) for _ in range(2)]

        def sems(prefix, names):
            return {n: sem(f"{prefix}_{n}") for n in names.split()}

        X = sems("x", "in0 in1 tr out ev sent0 sent1")
        NORM = sems("norm", "sq acc sum root rstd scaled hi lo")
        NORM_EVENTS = dict(sq=KB, acc=KB - 1, sum=1, root=1, rstd=1, scaled=KB, hi=KB, lo=KB)
        NORM_TO_PARTS = (True, False, True, True, False)
        SPLIT = sems("act_split", "in hi lo")
        S_Y1, S_Y2, S_PLE0, S_Y3, S_PLE1 = range(5)

        def norm_wait(eng, m, what, v):
            if v > 0:
                before = sum(NORM_TO_PARTS[:m]) if what in ("hi", "lo") else m
                eng.wait_ge(NORM[what], before * NORM_EVENTS[what] + v)

        IX = sems("idx", "sc scfree relu acc top sel bias biast biasd flip")
        GL = sems("gla", "in win keep last diff mmul logit x lsig cum eb q k kdexp kd kdt kdn a am s0 u su o oe "
                         "sq ms root rstd on ot gate y ysent pool pmm py psent z")
        PL = [sems(f"ple{m}", "in tr ev r h") for m in range(2)]
        AT = {k: sems(k, "aux gate sdone sread pre mx edone rden tdone te0 te1 pv oev ot y ysent")
              for k in ("dsa", "fox", "dil")}
        FC = sems("foxc", "x lsig cum sent t ev")
        xsent = sem("xsent")
        xback = sem("xback")
        windows = sem("pool_windows")

        block = ctx.enter_context(nc.Block())

        @block.sync
        def _(sp):
            def load(n, src, slot, cols=None):
                wait(sp, w_split, n - 1)
                dst = w_raw[:, slot]
                if cols is not None:
                    dst = dst[:, :, cols[0]:cols[1]]
                return sp.dma_start(dst, src)

            def whole(n, src, slot):
                load(n, src, slot).then_inc(w_loaded[slot], 16)

            def col(w, c):
                return w[:, :, c:c + P] if isinstance(c, int) else w[:, :, bass.ds(c, P)]

            n = 0
            whole(0, col(w_in, C_QI), 0)
            for r in range(4):
                load(1, w_in[:, :, C_KI:C_KI + 32], 1, (32 * r, 32 * r + 32)).then_inc(w_loaded[1], 16)
            load(2, w_in[:, :, C_WI:C_WI + 4], 0, (0, 4)).then_inc(w_loaded[0], 16)
            n = 3
            for c in (C_PU, C_PU + P, C_PG, C_PG + P):
                whole(n, col(w_in, c), n % 2)
                n += 1
            for base in (C_GQ, C_GK):
                for g in range(2):
                    for u in range(2):
                        c = base + (2 * g + u) * DK
                        load(n, w_in[:, :, c:c + DK], n % 2, (64 * u, 64 * u + DK)).then_inc(w_loaded[n % 2], 16)
                    n += 1
            for b in range(3):
                whole(n, col(w_in, C_GV + b * P), n % 2)
                n += 1
            load(n, w_in[:, :, C_GZ:C_GZ + 16], n % 2, (0, 16)).then_inc(w_loaded[n % 2], 16)
            n += 1
            for b in range(3):
                whole(n, col(w_in, C_GG + b * P), n % 2)
                n += 1
            assert n == N_FIRST
            with sp.Fori(0, 3) as it:
                for b, c in enumerate((C_DQ, C_DK, C_DV, C_DG)):
                    whole(W_DSA + b + it * 4, col(w_in, it * P + c), (W_DSA + b) % 2)

            def out_blocks(w, base):
                with sp.Fori(0, 4) as it:
                    for b in range(2):
                        whole(it * 2 + (base + b), col(w, it * (2 * P) + b * P), (base + b) % 2)

            def ple_blocks(m, base):
                for b in range(2):
                    wait(sp, w_split, base + b - 1)
                    dst = w_raw[:, (base + b) % 2].rearrange("p k c -> p (k c)").rearrange("p (k c) -> p k c", k=2)
                    sp.dma_start(dst, w_up[m][:, :, b * 512:(b + 1) * 512]).then_inc(w_loaded[(base + b) % 2], 16)
                out_blocks(w_gate[m], base + 2)

            if stop > 0:
                out_blocks(w_out[0], W_OUT1)
            if stop > 1:
                n = W_FOXF
                load(n, w_fox[:, :, 4 * D:4 * D + 16], n % 2, (0, 16)).then_inc(w_loaded[n % 2], 16)
                with sp.Fori(0, 8) as it:
                    for b in range(4):
                        whole(it * 4 + (W_FOX + b), col(w_fox, it * P + b * D), (W_FOX + b) % 2)
                out_blocks(w_out[1], W_OUT2)
                ple_blocks(0, W_PLE0)
            if stop > 2:
                with sp.Fori(0, 8) as it:
                    for b in range(10):
                        whole(it * 10 + (W_DIL + b), col(w_dil, it * P + b * D), (W_DIL + b) % 2)
                out_blocks(w_out[2], W_OUT3)
                ple_blocks(1, W_PLE1)

        w_total = {0: W_OUT1, 1: W_FOXF, 2: W_DIL}.get(stop, W_ALL)
        pieces = [1] * W_ALL
        pieces[1] = 4
        for n in range(7, 11):
            pieces[n] = 2

        def landed(n):
            return 16 * sum(pieces[m] for m in range(n % 2, n + 1, 2))

        @block.gpsimd
        def _(pool):
            def split(n, count, slot, passes):
                pool.wait_ge(w_loaded[slot], count)
                wait(pool, pass_done[1], passes)
                pool.tensor_tensor(w_hi[:, slot], w_raw[:, slot], ones[:, :].unsqueeze(1).broadcast_to([P, KB, P]),
                                   ALU.mult).then_inc(w_hi_done, 1)
                pool.wait_ge(w_hi_done, n + 1)
                pool.tensor_tensor(w_lo[:, slot], w_raw[:, slot], w_hi[:, slot].bitcast(F32),
                                   ALU.subtract).then_inc(w_split, 1)

            def passes_before(n):
                m = n - 2
                ends = m + 1
                for up in (W_PLE0, W_PLE1):
                    ends += 3 * min(max(m - up + 1, 0), 2)
                return ends

            def stretch(n0, n1):
                if n1 - n0 >= 2:
                    with pool.Fori(0, (n1 - n0) // 2) as it:
                        for b in range(2):
                            n = n0 + b
                            split(it * 2 + n, it * 16 + landed(n), n % 2, it * 2 + passes_before(n))
                if (n1 - n0) % 2:
                    split(n1 - 1, landed(n1 - 1), (n1 - 1) % 2, passes_before(n1 - 1))

            pool.wait_ge(consts, 16 * NCONST)
            for n in range(12):
                split(n, landed(n), n % 2, passes_before(n))
            edges = [12]
            for up in (W_PLE0, W_PLE1):
                if w_total > up + 2:
                    stretch(edges[-1], up + 2)
                    for n in (up + 2, up + 3):
                        split(n, landed(n), n % 2, passes_before(n))
                    edges.append(up + 4)
            stretch(edges[-1], w_total)

        @block.tensor
        def _(pe):
            def pass_T(n, c, slot, up=None, rows=None):
                for half in range(2):
                    if half == 0:
                        pe.wait_ge(w_split, n + 1)
                    wait(pe, pass_free[half], c)
                    kk = KB if up is None else 2
                    for k in range(kk):
                        if up is None:
                            hi, lo = w_hi[:, slot, k], w_lo[:, slot, k]
                        else:
                            hi, lo = (w[:, slot].rearrange("p k c -> p (k c)")[:, k * 512 + up * P:k * 512 + up * P + P]
                                      for w in (w_hi, w_lo))
                        tok = slice(half * 512, half * 512 + 512)
                        pe.matmul(proj[half][:, :], hi, act_hi[:, k, tok], start=(k == 0), stop=False)
                        pe.matmul(proj[half][:, :], hi, act_lo[:, k, tok], start=False, stop=False)
                        mm = pe.matmul(proj[half][:, :], lo, act_hi[:, k, tok], start=False, stop=(k == kk - 1))
                    mm.then_inc(pass_done[half], 1)

            def pass_N(n, c, slot, width=P):
                for half in range(2):
                    if half == 0:
                        pe.wait_ge(w_split, n + 1)
                    wait(pe, pass_free[half], c)
                    for t in range(4):
                        tok = slice((half * 4 + t) * P, (half * 4 + t + 1) * P)
                        out = proj[half][:, t * width:(t + 1) * width]
                        for k in range(KB):
                            hi, lo = w_hi[:, slot, k, 0:width], w_lo[:, slot, k, 0:width]
                            pe.matmul(out, act_hi[:, k, tok], hi, start=(k == 0), stop=False)
                            pe.matmul(out, act_hi[:, k, tok], lo, start=False, stop=False)
                            mm = pe.matmul(out, act_lo[:, k, tok], hi, start=False, stop=(k == KB - 1))
                    mm.then_inc(pass_done[half], 1)

            def norm_sum(m):
                norm_wait(pe, m, "acc", KB - 1)
                for half in range(2):
                    mm = pe.matmul(score[:, 0, half * 512:half * 512 + 512], ones[:, :],
                                   nacc[:, half * 512:half * 512 + 512], start=True, stop=True)
                mm.then_inc(NORM["sum"], 1)

            pe.wait_ge(consts, 16 * NCONST)
            for t in range(NT):
                pe.wait_ge(X[f"in{t % 2}"], 16 * (t // 2 + 1))
                if t >= 2:
                    pe.wait_ge(X["ev"], t - 1)
                for k in range(KB):
                    mm = pe.transpose(score[:, t % 2, k * P:(k + 1) * P], xnat[:, t % 2, k * P:(k + 1) * P], ident[:, :])
                mm.then_inc(X["tr"], 1)
            barrier(pe, 1)
            norm_sum(0)
            barrier(pe, 2)

            pass_T(0, 0, 0)
            pass_T(1, 1, 1)
            pass_N(2, 2, 0, width=4)
            pe.wait_ge(pass_free[0], 2)
            pe.wait_ge(pass_free[1], 2)
            count = 0

            def idx_scores(i):
                n = (i - 2) * IDX_H
                for h in range(IDX_H):
                    wait(pe, IX["relu"], n + h - 1)
                    for c in range(0, (i + 1) * P, 512):
                        w = min(512, (i + 1) * P - c)
                        mm = pe.matmul(score[:, h % 2, c:c + w], qiT[32 * h:32 * h + 32, i * P:(i + 1) * P],
                                       kiT[32 * h:32 * h + 32, c:c + w], start=True, stop=True,
                                       tile_position=(32 * h, 0))
                    mm.then_inc(IX["sc"], 1)

            pe.wait_ge(IX["bias"], 48)
            pe.matmul(obank[0:6, 0:384], gzT[0:32, 384:390], gzT[0:32, 0:384], start=True, stop=True).then_inc(IX["biast"], 1)
            pe.wait_ge(IX["biasd"], 16 * 7)
            for h in range(6):
                wait(pe, IX["flip"], h + 1)
                mm = pe.matmul(obank[:, 0:256], rel_s[:, 0, 0:P], work[:, 0:256] if h == 0 else
                               (rel_s[:, 0, P * 2:P * 4] if h == 1 else
                                rel_s[:, 0, P * 4:P * 6] if h == 2 else
                                rel_s[:, 0, P * 6:P * 8] if h == 3 else
                                rel_s[:, 1, 0:P * 2] if h == 4 else rel_s[:, 1, P * 2:P * 4]), start=True, stop=True)
                mm.then_inc(IX["biast"], 1)
            pe.wait_ge(IX["flip"], 7)
            for i in range(2, NT):
                idx_scores(i)
                for n in {2: (3, 4), 3: (5, 6), 4: (7, 8), 5: (9, 10), 6: (11, 12, 13), 7: (14, 15, 16, 17)}[i]:
                    (pass_N if 11 <= n <= 13 else pass_T)(n, n, n % 2)
            barrier(pe, 3)

            pe.wait_ge(GL["win"], 16 * 8)
            for g in range(2):
                for half in range(2):
                    mm = pe.matmul(score[:, g, half * 512:half * 512 + 512], gw2[0:16, g],
                                   gzT[0:16, half * 512:half * 512 + 512], start=True, stop=True)
            mm.then_inc(GL["logit"], 1)
            pe.wait_ge(GL["k"], 2)
            pe.wait_ge(GL["kd"], 2)
            n = 0
            for t in range(NT):
                for g in range(2):
                    tok = slice(t * P, (t + 1) * P)
                    wait(pe, GL["kdn"], n)
                    pe.transpose(proj[0][:, 0:P], gb_x[:, g, tok], ident[:, :]).then_inc(GL["kdt"], 1)
                    for u in range(2):
                        wait(pe, GL["am"], 2 * n + u)
                        pe.matmul(proj[1][:, 0:P] if u == 0 else score[:, 1, 512:512 + P],
                                  gk[64 * u:64 * u + DK, g, tok], gq[64 * u:64 * u + DK, g, tok],
                                  start=True, stop=True).then_inc(GL["a"], 1)
                    out = obank[:, 0:192]
                    wait(pe, GL["oe"], n)
                    for c in range(2):
                        ctok = slice(t * P + c * CH, t * P + (c + 1) * CH)
                        rows = slice(c * CH, (c + 1) * CH)
                        pe.wait_ge(GL["su"], 2 + 4 * n + 2 * c)
                        pe.matmul(obank[rows, 0:192], gq[:, g, ctok], state[:, g], start=True, stop=False,
                                  skip_group_check=True).then_inc(GL["s0"], 1)
                        pe.wait_ge(GL["kdn"], n + 1)
                        for hv in range(2):
                            for lo, b0, o0, w0 in value_cols(2 * g + hv):
                                mm = pe.matmul(score[:, 0, hv * DV + lo:hv * DV + lo + w0], kdN[rows, n % 2],
                                               gv[rows, b0, t, o0:o0 + w0], start=True, stop=True)
                        mm.then_inc(GL["u"], 1)
                    for hv in range(2):
                        pe.wait_ge(GL["am"], 2 * n + hv + 1)
                        for lo, b0, o0, w0 in value_cols(2 * g + hv):
                            mm = pe.matmul(obank[:, hv * DV + lo:hv * DV + lo + w0], intra[:, hv],
                                           gv[:, b0, t, o0:o0 + w0], start=False, stop=True, skip_group_check=True)
                    mm.then_inc(GL["o"], 1)
                    n += 1
            pe.wait_ge(GL["on"], 2)
            for b in range(3):
                wait(pe, GL["y"], b)
                for t in range(NT):
                    mm = pe.transpose(score[:, b % 2, t * P:(t + 1) * P], g_o[:, t, b * P:(b + 1) * P], ident[:, :])
                mm.then_inc(GL["ot"], 1)
            for b in range(2):
                pe.wait_ge(GL["pool"], b + 1)
                pe.wait_ge(GL["y"], 3)
                for half in range(2):
                    mm = pe.matmul(score[:, b, half * 512:half * 512 + 512], pw[:, b],
                                   pa[:, b, half * 512:half * 512 + 512], start=True, stop=True)
                mm.then_inc(GL["pmm"], 1)
            barrier(pe, 4)

            def attention(kind, it, heads):
                S, R = AT[kind], fields[kind]
                steps = attention_steps(kind)
                chunks = chunks_of(steps)
                starts = chunk_starts(chunks)
                C, NSTEP = starts[-1], len(steps)
                last_read = 0 if kind == "dil" else 1
                per = 1 if kind == "dil" else 2

                def scores(s):
                    i, hh, segs, _ = steps[s]
                    wait_turn(pe, S["sread"], it, NSTEP, s - last_read)
                    for g, buf, c0, j0, nb, _ in segs:
                        rows = slice(0, P) if kind == "dil" else slice(64 * hh, 64 * hh + 64)
                        c, end = c0, c0 + nb * P
                        while c < end:
                            w = min(512 - c % 512, end - c)
                            k0 = j0 * P + c - c0
                            mm = pe.matmul(score[:, buf, c:c + w], R["q"][g][rows, i * P:(i + 1) * P],
                                           R["k"][g][rows, k0:k0 + w], start=True, stop=True)
                            c += w
                    mm.then_inc(S["sdone"], 1)

                def turn(i):
                    s = per * (i + 1) - 1
                    pe.wait_ge(S["oev"], it * NSTEP + s + 1)
                    pe.transpose(obanks[s % 2][:, 256:384], R["o"][:, i % 2], ident[:, :]).then_inc(S["ot"], 1)

                scores(0)
                for s, (i, hh, segs, width) in enumerate(steps):
                    blocks = [(g, j0 + b) for g, _, _, j0, nb, _ in segs for b in range(nb)]
                    if s + 1 < NSTEP:
                        scores(s + 1)
                    if s and s % per == 0:
                        turn(i - 1)

                    def transposes(c):
                        q = starts[s] + c
                        b0, nb = chunks[s][c]
                        if c == 0:
                            pe.wait_ge(S["edone"], it * NSTEP + s + 1)
                        wait_turn(pe, S[f"te{q % 2}"], it, C // 2, q // 2)
                        for b in range(nb):
                            mm = pe.transpose(proj[q % 2][:, b * P:(b + 1) * P],
                                              R["p"][s % 2][:, (b0 + b) * P:(b0 + b + 1) * P], ident[:, :])
                        mm.then_inc(S["tdone"], 1)

                    def values(c):
                        q = starts[s] + c
                        b0, nb = chunks[s][c]
                        pe.wait_ge(S[f"te{q % 2}"], it * (C // 2) + q // 2 + 1)
                        if c == 0:
                            wait_turn(pe, S["oev"], it, NSTEP, s - 1)
                            wait_turn(pe, S["y"], it, NT, (s - 1) // per if (s - 1) % per == 0 else 0)
                        dh = P if kind == "dil" else 64
                        for b in range(nb):
                            g, j = blocks[b0 + b]
                            mm = pe.matmul(obanks[s % 2][:, 0:dh], R["pT"][:, q % 2, b * P:(b + 1) * P],
                                           R["v"][g][:, j, hh * 64:hh * 64 + dh],
                                           start=(b0 + b == 0), stop=(b0 + b == len(blocks) - 1))
                        mm.then_inc(S["pv"], 1)

                    transposes(0)
                    for c in range(1, len(chunks[s])):
                        transposes(c)
                        values(c - 1)
                    values(len(chunks[s]) - 1)
                turn(NT - 1)

            def mixer_loop(kind, iters, base, extra, order):
                with pe.Fori(0, iters) as it:
                    for b, form in enumerate(order):
                        n = it * len(order) + (base + b)
                        (pass_T if form == "T" else pass_N)(n, n + extra, (base + b) % 2)
                    for half in range(2):
                        pe.wait_ge(pass_free[half], it * len(order) + (base + extra + len(order)))
                    attention(kind, it, None)

            def out_loop(base, extra):
                with pe.Fori(0, 4) as it:
                    for b in range(2):
                        n = it * 2 + (base + b)
                        pass_T(n, n + extra, (base + b) % 2)

            def ple(m, base, extra, k):
                pe.wait_ge(PL[m]["in"], 16)
                for t in range(NT):
                    if t >= 2:
                        pe.wait_ge(PL[m]["ev"], t - 1)
                    for b in range(2):
                        mm = pe.transpose(score[:, t % 2, b * P:(b + 1) * P], pnat[:, t, b * P:(b + 1) * P], ident[:, :])
                    mm.then_inc(PL[m]["tr"], 1)
                pe.wait_ge(PL[m]["ev"], NT)
                for b in range(2):
                    for u in range(4):
                        pass_T(base + b, base + extra + 4 * b + u, (base + b) % 2, up=u)
                barrier(pe, k)
                pe.wait_ge(SPLIT["lo"], KB * ((S_PLE0, S_PLE1)[m] + 1))
                out_loop(base + 2, extra + PLE_EXTRA)
                barrier(pe, k + 1)

            mixer_loop("dsa", 3, W_DSA, 0, "TTNT")
            barrier(pe, 5)
            if stop > 0:
                pe.wait_ge(SPLIT["lo"], KB * (S_Y1 + 1))
                out_loop(W_OUT1, 0)
                barrier(pe, 6)
            if stop > 1:
                norm_sum(1)
                barrier(pe, 7)
                norm_sum(2)
                barrier(pe, 8)
                pass_T(W_FOXF, W_FOXF, W_FOXF % 2)
                pe.wait_ge(FC["cum"], 1)
                for t in range(NT):
                    mm = pe.transpose(obank[:, t * 16:t * 16 + 16], crow[0:16, t * P:(t + 1) * P], ident[0:16, 0:16])
                mm.then_inc(FC["t"], 1)
                pe.wait_ge(FC["ev"], 1)
                mixer_loop("fox", 8, W_FOX, 0, "TTNT")
                barrier(pe, 9)
                pe.wait_ge(SPLIT["lo"], KB * (S_Y2 + 1))
                out_loop(W_OUT2, 0)
                barrier(pe, 10)
                ple(0, W_PLE0, 0, 11)
            if stop > 2:
                norm_sum(3)
                barrier(pe, 13)
                mixer_loop("dil", 8, W_DIL, PLE_EXTRA, "TTTTTTNNNT")
                barrier(pe, 14)
                pe.wait_ge(SPLIT["lo"], KB * (S_Y3 + 1))
                out_loop(W_OUT3, PLE_EXTRA)
                barrier(pe, 15)
                ple(1, W_PLE1, PLE_EXTRA, 16)
                norm_sum(4)
                barrier(pe, 18)
            for t in range(NT):
                if t >= 2:
                    pe.wait_ge(X["out"], t - 1)
                for k in range(KB):
                    mm = pe.transpose(score[:, t % 2, k * P:(k + 1) * P], hT[:, k, t * P:(t + 1) * P], ident[:, :])
                mm.then_inc(X["tr"], 1)

        @block.scalar
        def _(act):
            def norm_act(m, into_parts):
                for k in range(KB):
                    norm_wait(act, m, "acc", k - 1)
                    act.activation(nsq[k % 2], hT[:, k], ACT.Square).then_inc(NORM["sq"], 1)
                norm_wait(act, m, "sum", 1)
                act.activation(nsq[0], score[:, 0], ACT.Sqrt, bias=epsc[:, 0:1], scale=1.0 / D).then_inc(NORM["root"], 1)
                if into_parts:
                    for k in range(KB):
                        norm_wait(act, m, "scaled", k + 1)
                        act.activation(act_hi[:, k], ntmp[k % 2], ACT.Copy).then_inc(NORM["hi"], 1)

            def split_act(src):
                for k in range(KB):
                    act.activation(act_hi[:, k], src[:, k], ACT.Copy).then_inc(SPLIT["hi"], 1)

            def evac(c, dst, scale=1.0, rows=slice(0, P), done=None, width=512):
                for half in range(2):
                    act.wait_ge(pass_done[half], c + 1)
                    ins = act.activation(dst[rows, half * width:(half + 1) * width], proj[half][rows, 0:width],
                                         ACT.Copy, scale=scale)
                    ins.then_inc(pass_free[half], 1)

            act.dma_start(ident[:, :], a["c_ident"]).then_inc(consts, 16)
            act.dma_start(ones[:, :], a["c_ones"]).then_inc(consts, 16)
            act.dma_start(diag[:, :], a["c_diag"]).then_inc(consts, 16)
            for m, name in enumerate(("norm_g", "final_norm_g", "fox_norm_2", "dil_norm_2", "final_norm_2")):
                v = a[name] if len(a[name].shape) == 1 else a[name][0]
                act.dma_start(gains[:, m], v.rearrange("(k p) -> p k", p=P), allow_slow_non_contiguous=True).then_inc(consts, 16)
            for t in range(NT):
                if t >= 2:
                    act.wait_ge(X["tr"], t - 1)
                act.dma_start(xnat[:, t % 2], a["x"][0, t * P:(t + 1) * P, :]).then_inc(X[f"in{t % 2}"], 16)
                if t >= 1:
                    act.wait_ge(X["tr"], t)
                    act.activation(hT[:, :, (t - 1) * P:t * P], score[:, (t - 1) % 2].rearrange("p (k c) -> p k c", c=P),
                                   ACT.Copy).then_inc(X["ev"], 1)
            act.wait_ge(X["tr"], NT)
            act.activation(hT[:, :, (NT - 1) * P:], score[:, (NT - 1) % 2].rearrange("p (k c) -> p k c", c=P),
                           ACT.Copy).then_inc(X["ev"], 1)
            act.wait_ge(X["ev"], NT)
            act.dma_start(xd, hT[:, :, :]).then_inc(xsent, 16)
            act.wait_ge(consts, 16 * NCONST)
            act.wait_ge(eps_set, 1)
            barrier(act, 1)
            norm_act(0, True)
            act.wait_ge(xsent, 16)
            barrier(act, 2)

            act.dma_start(gzT[0:32, 0:384], a["c_bucket"]).then_inc(IX["bias"], 16)
            act.dma_start(gzT[0:32, 384:390], a["rel_bias"]).then_inc(IX["bias"], 16)
            act.dma_start(rel_s[:, 0, 0:P], a["c_flip"]).then_inc(IX["bias"], 16)
            act.dma_start(rb31, a["rel_bias"][31:32, :].broadcast_to([P, 6])).then_inc(GL["in"], 16)
            act.dma_start(gnorm, a["gla_norm_g"].broadcast_to([P, DV])).then_inc(GL["in"], 16)
            act.dma_start(pscale, a["pool_scale"][0].rearrange("(b p) -> p b", p=P), allow_slow_non_contiguous=True).then_inc(GL["in"], 16)
            act.dma_start(amask, a["c_chunk"]).then_inc(GL["in"], 16)
            evac(0, qiT)
            evac(1, kiT)
            evac(2, wi_s.rearrange("p t h -> p (t h)"), scale=IDX_H ** -0.5, width=16)
            act.wait_ge(IX["biast"], 1)
            act.activation(work[0:6, 512:896], obank[0:6, 0:384], ACT.Copy).then_inc(IX["flip"], 1)
            act.wait_ge(IX["flip"], 1)
            act.dma_start(rd, work[0:6, 512:896]).then_inc(IX["biasd"], 16)
            act.wait_ge(IX["biasd"], 16)
            for h in range(6):
                dst = (work[:, 0:256], rel_s[:, 0, 256:512], rel_s[:, 0, 512:768], rel_s[:, 0, 768:1024],
                       rel_s[:, 1, 0:256], rel_s[:, 1, 256:512])[h]
                base = rd[h:h + 1, 0:256]
                src = bass.AP(tensor=base.tensor, offset=base.offset, ap=[[1, P], [1, 256]])
                act.dma_start(dst, src).then_inc(IX["biasd"], 16)
            act.wait_ge(GL["in"], 64)
            for h in range(6):
                act.wait_ge(IX["biast"], h + 2)
                act.activation(tbias[:, h], obank[:, 0:256], ACT.Copy).then_inc(IX["flip"], 1)

            def idx_relu(i):
                n = (i - 2) * IDX_H
                for h in range(IDX_H):
                    w = (i + 1) * P
                    act.wait_ge(IX["sc"], n + h + 1)
                    wait(act, IX["acc"], n + h - 1)
                    act.activation(rel_s[:, h % 2, 0:w], score[:, h % 2, 0:w], ACT.Relu,
                                   scale=IDX_D ** -0.5).then_inc(IX["relu"], 1)

            targets = {3: pu[:, 0], 4: pu[:, 1], 5: pg[:, 0], 6: pg[:, 1], 7: gq[:, 0], 8: gq[:, 1], 9: gk[:, 0],
                       10: gk[:, 1], 11: gv[:, 0].rearrange("p t c -> p (t c)"), 12: gv[:, 1].rearrange("p t c -> p (t c)"),
                       13: gv[:, 2].rearrange("p t c -> p (t c)"), 14: gzT, 15: gg[:, 0], 16: gg[:, 1], 17: gg[:, 2]}
            for i in range(2, NT):
                idx_relu(i)
                for n in {2: (3, 4), 3: (5, 6), 4: (7, 8), 5: (9, 10), 6: (11, 12, 13), 7: (14, 15, 16, 17)}[i]:
                    evac(n, targets[n], scale=DK ** -0.5 if n in (7, 8) else 1.0)
            barrier(act, 3)

            act.wait_ge(GL["z"], 3)
            for half in range(2):
                act.dma_start(gw2[0:16, :, 64 * half:64 * half + DK],
                              a["gla_gate_w2"][0].rearrange("r (g u c) -> u r g c", u=2, c=DK)[half]).then_inc(GL["win"], 16)
                act.dma_start(gb[64 * half:64 * half + DK, :],
                              a["gla_gate_b"][0].rearrange("(g u c) -> u c g", u=2, c=DK)[half], allow_slow_non_contiguous=True).then_inc(GL["win"], 16)
            for n in range(4):
                rows = slice(64 * (n % 2), 64 * (n % 2) + 64)
                act.dma_start(pw[rows, n // 2, rows], a["pool_w"][0, n]).then_inc(GL["win"], 16)
            act.dma_start(g_o.rearrange("p t c -> p (t c)")[:, 0:T], a["c_keep"]).then_inc(GL["keep"], 16)
            act.wait_ge(GL["x"], 2)
            act.activation(gb_e, gb_x, ACT.Abs).then_inc(GL["lsig"], 1)
            act.wait_ge(GL["lsig"], 1)
            act.activation(gb_e, gb_e, ACT.Exp, scale=-1.0).then_inc(GL["lsig"], 1)
            act.wait_ge(GL["lsig"], 2)
            act.activation(gb_e, gb_e, ACT.Ln, bias=1.0).then_inc(GL["lsig"], 1)
            act.wait_ge(GL["cum"], 2)
            act.activation(gb_e, gb_x, ACT.Exp, scale=1.0 / 16).then_inc(GL["eb"], 1)
            act.wait_ge(GL["q"], 3)
            act.activation(gb_e, gb_x, ACT.Exp, scale=-1.0 / 16).then_inc(GL["eb"], 1)
            act.wait_ge(GL["diff"], 2)
            act.activation(gb_x, gb_x, ACT.Exp, scale=1.0 / 16).then_inc(GL["kdexp"], 1)
            for n in range(2 * NT):
                act.wait_ge(GL["kdt"], n + 1)
                wait(act, GL["u"], 2 * (n - 1))
                act.activation(kdN[:, n % 2], proj[0][:, 0:P], ACT.Copy).then_inc(GL["kdn"], 1)
                act.wait_ge(GL["o"], n + 1)
                t, g = n // 2, n % 2
                act.activation(g_o[:, t, g * 192:(g + 1) * 192], obank[:, 0:192], ACT.Copy).then_inc(GL["oe"], 1)
            act.wait_ge(GL["ms"], 1)
            act.activation(g_ms[:, 0:32], g_ms[:, 0:32], ACT.Sqrt, bias=epsc[:, 0:1], scale=1.0 / DV).then_inc(GL["root"], 1)
            act.wait_ge(GL["on"], 2)
            for b in range(3):
                act.activation((gb_x[:, 0], gb_x[:, 1], gb_e[:, 0])[b], gg[:, b], ACT.Sigmoid).then_inc(GL["gate"], 1)
            for b in range(2):
                act.activation(gq[:, b], pg[:, b], ACT.Sigmoid).then_inc(GL["gate"], 1)
            for b in range(3):
                act.wait_ge(GL["y"], b + 1)
                act.dma_start(yd[b * P:(b + 1) * P, :], gg[:, b]).then_inc(GL["ysent"], 16)
            act.dma_start(pcnt, a["c_cnt"].rearrange("b p t -> p b t")).then_inc(GL["psent"], 16)
            for b in range(2):
                act.wait_ge(GL["py"], b + 1)
                act.dma_start(yd[(6 + b) * P:(7 + b) * P, :], pg[:, b]).then_inc(GL["ysent"], 16)
            act.wait_ge(GL["ysent"], 16 * 5)
            barrier(act, 4)

            def attention(kind, it):
                S, R = AT[kind], fields[kind]
                steps = attention_steps(kind)
                chunks = chunks_of(steps)
                starts = chunk_starts(chunks)
                C, NSTEP = starts[-1], len(steps)
                for s, (i, hh, segs, width) in enumerate(steps):
                    act.wait_ge(S["mx"], it * NSTEP + s + 1)
                    act.activation(R["p"][s % 2][:, 0:width], R["p"][s % 2][:, 0:width], ACT.Exp,
                                   bias=R["st"][:, s:s + 1], accum_out=R["st"][:, 16 + s:17 + s]).then_inc(S["edone"], 1)
                    for c, (b0, nb) in enumerate(chunks[s]):
                        q = starts[s] + c
                        if q % 2:
                            act.wait_ge(S["tdone"], it * C + q + 1)
                            wait_turn(act, S["pv"], it, C, q - 1)
                            act.activation(R["pT"][:, 1, 0:nb * P], proj[1][:, 0:nb * P], ACT.Copy).then_inc(S["te1"], 1)

            def mixer_loop(kind, iters, base, extra, order, rows):
                S, R = AT[kind], fields[kind]
                scale = 128 ** -0.5 if kind == "dil" else 0.125
                ng = 3 if kind == "dil" else 1
                with act.Fori(0, iters) as it:
                    if kind == "fox":
                        for hh in range(2):
                            act.dma_start(cB[hh], cd[bass.ds(it * 2 + hh, 1), :].broadcast_to([P, T])).then_inc(S["aux"], 16)
                    dsts = R["q"] + R["k"] + [v.rearrange("p t c -> p (t c)") for v in R["v"]] + [R["g"]]
                    for b, dst in enumerate(dsts):
                        c = it * len(order) + (base + extra + b)
                        for half in range(2):
                            act.wait_ge(pass_done[half], c + 1)
                            cols = slice(half * 512, half * 512 + 512)
                            act.activation(dst[:, cols], proj[half][:, :], ACT.Copy, scale=scale if b < ng else 1.0)\
                               .then_inc(pass_free[half], 1)
                    for half in range(2):
                        act.wait_ge(pass_free[half], it * len(order) + (base + extra + len(order)))
                    act.activation(R["e"], R["g"], ACT.Sigmoid).then_inc(S["gate"], 1)
                    attention(kind, it)
                    act.wait_ge(S["y"], it * NT + NT)
                    act.dma_start(yd[bass.ds(it * P + rows, P), :], R["y"]).then_inc(S["ysent"], 16)
                    act.wait_ge(S["ysent"], it * 16 + 16)

            def load_y(mixer):
                for k in range(KB):
                    act.dma_start(yin[:, k], yd[k * P:(k + 1) * P, :]).then_inc(SPLIT["in"], 16)
                act.wait_ge(SPLIT["in"], 16 * KB * (mixer + 1))
                split_act(yin)

            def ple(m, base, extra, k):
                act.dma_start(pnat, a["p_2"][m, 0].rearrange("(t p) c -> p t c", p=P)).then_inc(PL[m]["in"], 16)
                for t in range(NT):
                    act.wait_ge(PL[m]["tr"], t + 1)
                    act.activation(act_hi[:, 0:2, t * P:(t + 1) * P],
                                   score[:, t % 2, 0:256].rearrange("p (b c) -> p b c", b=2), ACT.Copy).then_inc(PL[m]["h"], 1)
                for cb in range(8):
                    evac(base + extra + cb, upT[:, cb])
                barrier(act, k)
                split_act(hT)
                with act.Fori(0, 4) as it:
                    for b in range(2):
                        for half in range(2):
                            c = it * 2 + (base + 2 + extra + PLE_EXTRA + b)
                            act.wait_ge(pass_done[half], c + 1)
                            act.wait_ge(PL[m]["r"], it * 8 + (4 * b + 2 * half + 6))
                            act.activation(ple_e[half], proj[half][:, :], ACT.Sigmoid).then_inc(pass_free[half], 1)
                barrier(act, k + 1)

            mixer_loop("dsa", 3, W_DSA, 0, "TTNT", 3 * P)
            act.dma_start(hT[:, :, :], xd).then_inc(xback, 16)
            act.wait_ge(xback, 16)
            barrier(act, 5)
            if stop > 0:
                load_y(0)
                barrier(act, 6)
            if stop > 1:
                norm_act(1, False)
                barrier(act, 7)
                norm_act(2, True)
                barrier(act, 8)
                act.dma_start(fb[0:16, 0:1], a["fox_b_f_2"][0].rearrange("(h o) -> h o", o=1), allow_slow_non_contiguous=True).then_inc(FC["x"], 16)
                evac(W_FOXF, crow, rows=slice(0, 16))
                act.wait_ge(FC["x"], 17)
                act.activation(ctmp[0:16], crow[0:16], ACT.Abs).then_inc(FC["lsig"], 1)
                act.wait_ge(FC["lsig"], 1)
                act.activation(ctmp[0:16], ctmp[0:16], ACT.Exp, scale=-1.0).then_inc(FC["lsig"], 1)
                act.wait_ge(FC["lsig"], 2)
                act.activation(ctmp[0:16], ctmp[0:16], ACT.Ln, bias=1.0).then_inc(FC["lsig"], 1)
                act.wait_ge(FC["cum"], 1)
                act.dma_start(cd, crow[0:16]).then_inc(FC["sent"], 16)
                act.wait_ge(FC["sent"], 16)
                mixer_loop("fox", 8, W_FOX, 0, "TTNT", 0)
                barrier(act, 9)
                load_y(1)
                barrier(act, 10)
                ple(0, W_PLE0, 0, 11)
            if stop > 2:
                norm_act(3, True)
                barrier(act, 13)
                act.dma_start(cdist, a["c_dist"]).then_inc(AT["dil"]["aux"], 16)
                act.dma_start(cslope, a["c_slope"]).then_inc(AT["dil"]["aux"], 16)
                mixer_loop("dil", 8, W_DIL, PLE_EXTRA, "TTTTTTNNNT", 0)
                barrier(act, 14)
                load_y(2)
                barrier(act, 15)
                ple(1, W_PLE1, PLE_EXTRA, 16)
                norm_act(4, False)
                barrier(act, 18)
            for t in range(NT):
                act.wait_ge(X["tr"], NT + t + 1)
                if t >= 2:
                    act.wait_ge(X[f"sent{t % 2}"], 16 * (t // 2))
                act.activation(xnat[:, t % 2], score[:, t % 2], ACT.Copy).then_inc(X["out"], 1)
                act.wait_ge(X["out"], t + 1)
                act.dma_start(a["out"][0, t * P:(t + 1) * P, :], xnat[:, t % 2]).then_inc(X[f"sent{t % 2}"], 16)
            for slot in range(2):
                act.wait_ge(X[f"sent{slot}"], 16 * (NT // 2))

        @block.vector
        def _(dve):
            def norm_dve(m, into_parts):
                for k in range(1, KB):
                    norm_wait(dve, m, "sq", k + 1)
                    if k > 1:
                        norm_wait(dve, m, "acc", k - 1)
                    dve.tensor_tensor(nacc, nsq[0] if k == 1 else nacc, nsq[k % 2], ALU.add).then_inc(NORM["acc"], 1)
                norm_wait(dve, m, "root", 1)
                dve.reciprocal(nacc, nsq[0]).then_inc(NORM["rstd"], 1)
                norm_wait(dve, m, "rstd", 1)
                for k in range(KB):
                    if into_parts:
                        if k >= 2:
                            norm_wait(dve, m, "lo", k - 1)
                        dve.scalar_tensor_tensor(ntmp[k % 2], hT[:, k], gains[:, m, k:k + 1], nacc, ALU.mult, ALU.mult)\
                           .then_inc(NORM["scaled"], 1)
                        norm_wait(dve, m, "hi", k + 1)
                        dve.tensor_tensor(act_lo[:, k], ntmp[k % 2], act_hi[:, k].bitcast(F32), ALU.subtract)\
                           .then_inc(NORM["lo"], 1)
                    else:
                        dve.scalar_tensor_tensor(hT[:, k], hT[:, k], gains[:, m, k:k + 1], nacc, ALU.mult, ALU.mult)\
                           .then_inc(NORM["scaled"], 1)

            def split_dve(m, src):
                for k in range(KB):
                    dve.wait_ge(SPLIT["hi"], m * KB + k + 1)
                    dve.tensor_tensor(act_lo[:, k], src[:, k], act_hi[:, k].bitcast(F32), ALU.subtract)\
                       .then_inc(SPLIT["lo"], 1)

            dve.memset(epsc[:, :], EPS).then_inc(eps_set, 1)
            barrier(dve, 1)
            norm_dve(0, True)
            barrier(dve, 2)

            dve.wait_ge(pass_free[0], 3)
            dve.wait_ge(pass_free[1], 3)
            dve.wait_ge(IX["flip"], 7)
            dve.wait_ge(GL["in"], 64)
            for h in range(6):
                dve.tensor_scalar(tbias[:, h], tbias[:, h], rb31[:, h:h + 1], None, ALU.subtract).then_inc(IX["bias"], 1)
            sel = 0
            for i in range(2):
                if i:
                    dve.memset(maskb[:, mask_offset(i):mask_offset(i) + P * i], 0.0).then_inc(IX["sel"], 1)
                    sel += 1
                dve.tensor_copy(maskb[:, mask_offset(i) + P * i:mask_offset(i + 1)], diag[:, :]).then_inc(IX["sel"], 1)
                sel += 1
            top = 0
            for i in range(2, NT):
                n = (i - 2) * IDX_H
                w = (i + 1) * P
                for h in range(IDX_H):
                    dve.wait_ge(IX["relu"], n + h + 1)
                    if h == 0:
                        wait(dve, IX["sel"], sel)
                        dve.tensor_scalar(work[:, 0:w], rel_s[:, 0, 0:w], wi_s[:, i, 0:1], None, ALU.mult)\
                           .then_inc(IX["acc"], 1)
                    else:
                        dve.wait_ge(IX["acc"], n + h)
                        dve.scalar_tensor_tensor(work[:, 0:w], rel_s[:, h % 2, 0:w], wi_s[:, i, h:h + 1], work[:, 0:w],
                                                 ALU.mult, ALU.add).then_inc(IX["acc"], 1)
                dve.wait_ge(IX["acc"], n + IDX_H)
                dve.tensor_tensor(work[:, i * P:w], work[:, i * P:w], diag[:, :], ALU.add).then_inc(IX["top"], 1)
                top += 1
                for r in range(TOPK // 8):
                    dve.wait_ge(IX["top"], top)
                    dve.max(top8, work[:, 0:w]).then_inc(IX["top"], 1)
                    dve.wait_ge(IX["top"], top + 1)
                    dve.match_replace(work[:, 0:w], top8, work[:, 0:w], -3e38).then_inc(IX["top"], 1)
                    top += 2
                dve.wait_ge(IX["top"], top)
                dve.tensor_scalar(maskb[:, mask_offset(i):mask_offset(i + 1)], work[:, 0:w], -2e38, NEG,
                                  ALU.is_gt, ALU.mult).then_inc(IX["sel"], 1)
                sel += 1
            for pad in (gw2, gb, pw):
                dve.memset(pad, 0.0).then_inc(GL["z"], 1)
            barrier(dve, 3)

            g = GL
            dve.memset(state, 0.0).then_inc(g["su"], 1)
            dve.memset(intra, 0.0).then_inc(g["su"], 1)
            dve.wait_ge(g["win"], 16 * 8)
            dve.wait_ge(g["logit"], 1)
            for b in range(2):
                dve.tensor_scalar(gb_x[:, b], score[:, b], gb[:, b:b + 1], None, ALU.add).then_inc(g["x"], 1)
            dve.wait_ge(g["lsig"], 3)
            for b in range(2):
                dve.scalar_tensor_tensor(gb_x[:, b], gb_x[:, b], 0.0, gb_e[:, b], ALU.min, ALU.subtract).then_inc(g["lsig"], 1)
            dve.wait_ge(g["lsig"], 5)
            dve.wait_ge(g["keep"], 16)
            for b in range(2):
                dve.tensor_tensor_scan(gb_x[:, b], g_o.rearrange("p t c -> p (t c)")[:, 0:T], gb_x[:, b], 0.0,
                                       ALU.mult, ALU.add).then_inc(g["cum"], 1)
            dve.wait_ge(g["eb"], 1)
            for b in range(2):
                dve.tensor_tensor(gq[:, b], gq[:, b], gb_e[:, b], ALU.mult).then_inc(g["q"], 1)
            dve.tensor_copy(dec, gb_e.rearrange("p g (c j) -> p g c j", j=CH)[:, :, :, CH - 1]).then_inc(g["q"], 1)
            dve.wait_ge(g["cum"], 2)
            for b in range(2):
                dve.tensor_copy(g_ms[:, b * 16:b * 16 + 16], gb_x[:, b].rearrange("p (c j) -> p c j", j=CH)[:, :, CH - 1])\
                   .then_inc(g["last"], 1)
            dve.wait_ge(g["last"], 2)
            dve.wait_ge(g["eb"], 2)
            for b in range(2):
                x3 = gb_x[:, b].rearrange("p (c j) -> p c j", j=CH)
                dve.tensor_tensor(x3, g_ms[:, b * 16:b * 16 + 16].unsqueeze(2).broadcast_to([P, 16, CH]), x3,
                                  ALU.subtract).then_inc(g["diff"], 1)
            dve.wait_ge(g["kdexp"], 1)
            for b in range(2):
                dve.tensor_tensor(gb_x[:, b], gb_x[:, b], gk[:, b], ALU.mult).then_inc(g["kd"], 1)
            dve.wait_ge(g["kd"], 2)
            for b in range(2):
                dve.tensor_tensor(gk[:, b], gk[:, b], gb_e[:, b], ALU.mult).then_inc(g["k"], 1)
            dve.wait_ge(g["su"], 2)
            for n in range(2 * NT):
                t, b = n // 2, n % 2
                for u in range(2):
                    dve.wait_ge(g["a"], 2 * n + u + 1)
                    wait(dve, g["o"], n)
                    dve.copy_predicated(intra[:, u], amask, proj[1][:, 0:P] if u == 0 else score[:, 1, 512:512 + P])\
                       .then_inc(g["am"], 1)
                for c in range(2):
                    dve.wait_ge(g["u"], 2 * n + c + 1)
                    dve.wait_ge(g["su"], 2 + 4 * n + 2 * c)
                    for u in range(2):
                        rows, cols = slice(64 * u, 64 * u + DK), slice(u * DV, (u + 1) * DV)
                        dve.scalar_tensor_tensor(state[rows, b, cols], state[rows, b, cols],
                                                 dec[rows, b, 2 * t + c:2 * t + c + 1], score[rows, 0, cols],
                                                 ALU.mult, ALU.add).then_inc(g["su"], 1)
            dve.wait_ge(g["oe"], 2 * NT)
            o_flat = g_o.rearrange("p t c -> p (t c)")
            o3 = o_flat.rearrange("p (n v) -> p n v", v=DV)
            sq = arena[:, at_tmp:at_tmp + 3 * T]
            dve.tensor_tensor(sq, o_flat, o_flat, ALU.mult).then_inc(g["sq"], 1)
            dve.wait_ge(g["sq"], 1)
            dve.tensor_reduce(g_ms[:, 0:32], sq.rearrange("p (n v) -> p n v", v=DV), AX.X, ALU.add).then_inc(g["ms"], 1)
            dve.wait_ge(g["root"], 1)
            dve.reciprocal(g_ms[:, 32:64], g_ms[:, 0:32]).then_inc(g["rstd"], 1)
            dve.wait_ge(g["rstd"], 1)
            dve.tensor_tensor(o3, o3, g_ms[:, 32:64].unsqueeze(2).broadcast_to([P, 32, DV]), ALU.mult).then_inc(g["on"], 1)
            dve.wait_ge(g["on"], 1)
            dve.tensor_tensor(o3, o3, gnorm.unsqueeze(1).broadcast_to([P, 32, DV]), ALU.mult).then_inc(g["on"], 1)
            es = [gb_x[:, 0], gb_x[:, 1], gb_e[:, 0], gq[:, 0], gq[:, 1]]
            zs = [gg[:, 0], gg[:, 1], gg[:, 2], pg[:, 0], pg[:, 1]]
            for n in range(5):
                dve.wait_ge(g["gate"], n + 1)
                dve.tensor_tensor(zs[n], zs[n], es[n], ALU.mult).then_inc(g["mmul"], 1)
            for b in range(3):
                dve.wait_ge(g["ot"], b + 1)
                dve.wait_ge(g["mmul"], b + 1)
                dve.tensor_tensor(gg[:, b], score[:, b % 2], gg[:, b], ALU.mult).then_inc(g["y"], 1)

            dve.wait_ge(g["mmul"], 5)
            dve.wait_ge(g["y"], 3)
            dve.tensor_copy(pa[:, :, 0:1], pu[:, :, 0:1]).then_inc(windows, 1)
            dve.tensor_tensor(pa[:, :, 1:T], pu[:, :, 1:T], pu[:, :, 0:T - 1], ALU.add).then_inc(windows, 1)
            dve.wait_ge(windows, 2)
            dve.tensor_copy(pb[:, :, 0:2], pa[:, :, 0:2]).then_inc(windows, 1)
            dve.tensor_tensor(pb[:, :, 2:T], pa[:, :, 2:T], pa[:, :, 0:T - 2], ALU.add).then_inc(windows, 1)
            dve.wait_ge(windows, 4)
            dve.tensor_copy(pa[:, 1, 0:4], pb[:, 1, 0:4]).then_inc(windows, 1)
            dve.tensor_tensor(pa[:, 1, 4:T], pb[:, 1, 4:T], pb[:, 1, 0:T - 4], ALU.add).then_inc(windows, 1)
            dve.wait_ge(windows, 6)
            dve.tensor_copy(pb[64:P, 1, 0:8], pa[64:P, 1, 0:8]).then_inc(windows, 1)
            dve.tensor_tensor(pb[64:P, 1, 8:T], pa[64:P, 1, 8:T], pa[64:P, 1, 0:T - 8], ALU.add).then_inc(windows, 1)
            dve.wait_ge(g["psent"], 16)
            dve.wait_ge(windows, 8)
            for b in range(2):
                dve.tensor_tensor(pa[0:64, b], pa[0:64, b], pcnt[0:64, b], ALU.mult).then_inc(windows, 1)
                dve.tensor_tensor(pa[64:P, b], pb[64:P, b], pcnt[64:P, b], ALU.mult).then_inc(windows, 1)
            for b in range(2):
                dve.wait_ge(windows, 8 + 2 * b + 2)
                dve.tensor_tensor(pa[:, b], pa[:, b], pu[:, b], ALU.subtract).then_inc(g["pool"], 1)
            for b in range(2):
                dve.wait_ge(g["pmm"], b + 1)
                dve.scalar_tensor_tensor(pg[:, b], score[:, b], pscale[:, b:b + 1], pg[:, b], ALU.mult, ALU.mult)\
                   .then_inc(g["py"], 1)
            barrier(dve, 4)

            def attention(kind, it):
                S, R = AT[kind], fields[kind]
                steps = attention_steps(kind)
                chunks = chunks_of(steps)
                starts = chunk_starts(chunks)
                C, NSTEP = starts[-1], len(steps)
                per = 1 if kind == "dil" else 2
                npre = 3 if kind == "dil" else 1

                def rows(s):
                    i, hh, segs, width = steps[s]
                    row = R["p"][s % 2]
                    dve.wait_ge(S["sdone"], it * NSTEP + s + 1)
                    wait_turn(dve, S["tdone"], it, C, starts[max(s - 1, 0)])
                    for n, (g_, buf, c0, j0, nb, col) in enumerate(segs):
                        src = score[:, buf, c0:c0 + nb * P]
                        dst = row[:, col:col + nb * P]
                        last = n == len(segs) - 1
                        if kind == "dil":
                            at = sum(DIL_NB[:g_ + 1]) * P
                            ins = dve.scalar_tensor_tensor(dst, cdist[:, at - nb * P:at], cslope[:, bass.ds(it + 8 * g_, 1)],
                                                           src, ALU.mult, ALU.add)
                        elif kind == "fox":
                            ins = dve.scalar_tensor_tensor(dst, src, ccol[:, i, bass.ds(it * 2 + hh, 1)],
                                                           cB[hh][:, 0:width], ALU.add, ALU.subtract)
                        else:
                            ins = dve.scalar_tensor_tensor(dst, src, rb31[:, bass.ds(it * 2 + hh, 1)],
                                                           maskb[:, mask_offset(i):mask_offset(i + 1)], ALU.add, ALU.add)
                        ins.then_inc(S["sread"] if last else S["pre"], 1)
                    dve.wait_ge(S["sread"], it * NSTEP + s + 1)
                    if kind == "dil":
                        dve.wait_ge(S["pre"], it * (2 * NSTEP) + 2 * s + 2)
                    elif kind == "fox":
                        dve.tensor_tensor(row[:, width - P:width], row[:, width - P:width], diag[:, :], ALU.add)\
                           .then_inc(S["pre"], 1)
                        dve.wait_ge(S["pre"], it * NSTEP + s + 1)
                    else:
                        w = min(width, 2 * P)
                        near = tbias[:, bass.ds(it * 2 + hh, 1), 2 * P - w:2 * P].rearrange("p o c -> p (o c)")
                        dve.tensor_tensor(row[:, width - w:width], row[:, width - w:width], near, ALU.add)\
                           .then_inc(S["pre"], 1)
                        dve.wait_ge(S["pre"], it * NSTEP + s + 1)
                    dve.tensor_reduce(R["st"][:, s:s + 1], row[:, 0:width], AX.X, ALU.max, negate=True)\
                       .then_inc(S["mx"], 1)

                def finish(i):
                    dve.wait_ge(S["ot"], it * NT + i + 1)
                    dve.tensor_tensor(R["y"][:, i * P:(i + 1) * P], obanks[(per * (i + 1) - 1) % 2][:, 256:384], R["g"][:, i * P:(i + 1) * P],
                                      ALU.mult).then_inc(S["y"], 1)

                rows(0)
                dve.wait_ge(S["gate"], it * 2 + 1)
                dve.tensor_tensor(R["g"], R["g"], R["e"], ALU.mult).then_inc(S["gate"], 1)
                dve.wait_ge(S["gate"], it * 2 + 2)
                for s, (i, hh, segs, width) in enumerate(steps):
                    if s + 1 < NSTEP:
                        rows(s + 1)
                    if s and s % per == 0:
                        finish(i - 1)
                    for c, (b0, nb) in enumerate(chunks[s]):
                        q = starts[s] + c
                        if q % 2 == 0:
                            dve.wait_ge(S["tdone"], it * C + q + 1)
                            wait_turn(dve, S["pv"], it, C, q - 1)
                            dve.tensor_copy(R["pT"][:, 0, 0:nb * P], proj[0][:, 0:nb * P]).then_inc(S["te0"], 1)
                    dve.wait_ge(S["edone"], it * NSTEP + s + 1)
                    dve.reciprocal(R["st"][:, 32 + s:33 + s], R["st"][:, 16 + s:17 + s]).then_inc(S["rden"], 1)
                    dve.wait_ge(S["rden"], it * NSTEP + s + 1)
                    dve.wait_ge(S["pv"], it * C + starts[s + 1])
                    if hh == 0:
                        wait_turn(dve, S["ot"], it, NT, i - 1)
                    dh = P if kind == "dil" else 64
                    dve.tensor_scalar(R["o"][:, i % 2, hh * 64:hh * 64 + dh], obanks[s % 2][:, 0:dh],
                                      R["st"][:, 32 + s:33 + s], None, ALU.mult).then_inc(S["oev"], 1)
                finish(NT - 1)

            def mixer_loop(kind, iters):
                with dve.Fori(0, iters) as it:
                    if kind == "fox":
                        dve.wait_ge(AT[kind]["aux"], it * 32 + 32)
                    attention(kind, it)

            def res(c):
                return lambda half: hT[:, bass.ds(c, 1), half * 512:half * 512 + 512].rearrange("p o c -> p (o c)")

            def out_loop(base, extra):
                with dve.Fori(0, 4) as it:
                    for b in range(2):
                        for half in range(2):
                            dve.wait_ge(pass_done[half], it * 2 + (base + extra + b + 1))
                            h = res(it * 2 + b)(half)
                            dve.tensor_tensor(h, h, proj[half][:, :], ALU.add).then_inc(pass_free[half], 1)

            def ple(m, k):
                s = PL[m]
                for t in range(NT):
                    dve.wait_ge(s["h"], t + 1)
                    dve.tensor_tensor(act_lo[:, 0:2, t * P:(t + 1) * P],
                                      score[:, t % 2, 0:256].rearrange("p (b c) -> p b c", b=2),
                                      act_hi[:, 0:2, t * P:(t + 1) * P].bitcast(F32), ALU.subtract).then_inc(s["ev"], 1)
                barrier(dve, k)
                split_dve((S_PLE0, S_PLE1)[m], hT)
                dve.wait_ge(SPLIT["lo"], KB * ((S_PLE0, S_PLE1)[m] + 1))
                dve.drain().then_inc(s["r"], 8)
                base = (W_PLE0, W_PLE1)[m] + 2 + PLE_EXTRA * (m + 1)
                with dve.Fori(0, 4) as it:
                    for b in range(2):
                        for half in range(2):
                            n = it * 8 + (8 + 4 * b + 2 * half)
                            e, t = ple_e[half], ple_t[half]
                            u = upT[:, bass.ds(it * 2 + b, 1), half * 512:half * 512 + 512].rearrange("p o c -> p (o c)")
                            dve.wait_ge(pass_free[half], it * 2 + (base + b + 1))
                            dve.tensor_tensor(t, u, e, ALU.mult).then_inc(s["r"], 1)
                            dve.wait_ge(s["r"], n + 1)
                            h = res(it * 2 + b)(half)
                            dve.tensor_tensor(h, h, t, ALU.add).then_inc(s["r"], 1)
                barrier(dve, k + 1)

            mixer_loop("dsa", 3)
            barrier(dve, 5)
            if stop > 0:
                split_dve(S_Y1, yin)
                out_loop(W_OUT1, 0)
                barrier(dve, 6)
            if stop > 1:
                norm_dve(1, False)
                barrier(dve, 7)
                norm_dve(2, True)
                barrier(dve, 8)
                dve.wait_ge(pass_free[0], W_FOXF + 1)
                dve.wait_ge(pass_free[1], W_FOXF + 1)
                dve.wait_ge(FC["x"], 16)
                dve.tensor_scalar(crow[0:16], crow[0:16], fb[0:16, 0:1], None, ALU.add).then_inc(FC["x"], 1)
                dve.wait_ge(FC["lsig"], 3)
                dve.scalar_tensor_tensor(crow[0:16], crow[0:16], 0.0, ctmp[0:16], ALU.min, ALU.subtract).then_inc(FC["lsig"], 1)
                dve.wait_ge(FC["lsig"], 4)
                dve.memset(ctmp[0:16], 1.0).then_inc(FC["lsig"], 1)
                dve.wait_ge(FC["lsig"], 5)
                dve.tensor_tensor_scan(crow[0:16], ctmp[0:16], crow[0:16], 0.0, ALU.mult, ALU.add).then_inc(FC["cum"], 1)
                dve.wait_ge(FC["t"], 1)
                dve.tensor_copy(ccol.rearrange("p t h -> p (t h)"), obank[:, 0:128]).then_inc(FC["ev"], 1)
                dve.wait_ge(FC["ev"], 1)
                mixer_loop("fox", 8)
                barrier(dve, 9)
                split_dve(S_Y2, yin)
                out_loop(W_OUT2, 0)
                barrier(dve, 10)
                ple(0, 11)
            if stop > 2:
                norm_dve(3, True)
                barrier(dve, 13)
                dve.wait_ge(AT["dil"]["aux"], 32)
                mixer_loop("dil", 8)
                barrier(dve, 14)
                split_dve(S_Y3, yin)
                out_loop(W_OUT3, PLE_EXTRA)
                barrier(dve, 15)
                ple(1, 16)
                norm_dve(4, False)
                barrier(dve, 18)


_INS = ["x", "norm_g", "w_in", "gla_gate_w2", "gla_gate_b", "gla_norm_g", "rel_bias", "pool_w", "pool_scale", "w_out",
        "final_norm_g", "p_2", "fox_norm_2", "fox_w_in_2", "fox_b_f_2", "fox_w_out_2", "dil_norm_2", "dil_w_in_2",
        "dil_w_out_2", "ple_w_up_2", "ple_w_gate_2", "final_norm_2"]


def kernel(**inputs):
    import concourse.bacc as bacc
    from concourse.bass_utils import run_bass_kernel_spmd

    nc = bacc.Bacc("TRN2", target_bir_lowering=False, num_devices=1)
    arrays, a = {}, {}
    given = {name: np.ascontiguousarray(inputs[name]) for name in _INS}
    given.update(host_constants())
    for name, x in given.items():
        arrays[name + "_dram"] = x
        a[name] = nc.dram_tensor(name + "_dram", x.shape, mybir.dt.from_np(x.dtype), kind="ExternalInput").ap()
    a["out"] = nc.dram_tensor("out_dram", (1, T, D), F32, kind="ExternalOutput").ap()
    build(nc, a)
    r = run_bass_kernel_spmd(nc, [arrays], core_ids=[0])
    return r.results[0]["out_dram"]
```

```python
from contextlib import ExitStack
import math

import numpy as np
import concourse.bass as bass
from concourse import mybir

F32 = mybir.dt.float32
F32R = mybir.dt.float32r
BF16 = mybir.dt.bfloat16
I32 = mybir.dt.int32
ALU = mybir.AluOpType
ACT = mybir.ActivationFunctionType
AX = mybir.AxisListType

P = 128
T = 1024
D = 1024
KB = D // P
NT = T // P
EPS = 1e-6
NEG = -1e30

GH, DK, DV, CH = 4, 48, 96, 64
SIZES = (GH * DK, GH * DK, GH * DV, 16, GH * DV, 384, 384, 384, 384, 128, 32, 4, 256, 256)
OFF = [sum(SIZES[:n]) for n in range(len(SIZES))]
(C_GQ, C_GK, C_GV, C_GZ, C_GG, C_DQ, C_DK, C_DV, C_DG, C_QI, C_KI, C_WI, C_PU, C_PG) = OFF
TOPK = 256
IDX_H, IDX_D = 4, 32
DIL_PATTERN = ((128, 1), (512, 4), (2048, 16))
DIL_NB = [min(w // P + 1, NT) for w, _ in DIL_PATTERN]

N_FIRST = 18
W_DSA = N_FIRST
W_OUT1 = W_DSA + 3 * 4
W_FOXF = W_OUT1 + 8
W_FOX = W_FOXF + 1
W_OUT2 = W_FOX + 8 * 4
W_PLE0 = W_OUT2 + 8
W_DIL = W_PLE0 + 10
W_OUT3 = W_DIL + 8 * 10
W_PLE1 = W_OUT3 + 8
W_ALL = W_PLE1 + 10
PLE_EXTRA = 6


def attention_steps(kind):
    steps = []
    if kind == "dil":
        for i in range(NT):
            segs, col = [], 0
            for g, buf, c0 in ((2, 0, 0), (0, 1, 0), (1, 1, 256)):
                nb = min(DIL_NB[g], i + 1)
                segs.append((g, buf, c0, i + 1 - nb, nb, col))
                col += nb * P
            steps.append((i, 0, segs, col))
    else:
        for s in range(2 * NT):
            i = s // 2
            steps.append((i, s % 2, [(0, 0, 0, 0, i + 1, 0)], (i + 1) * P))
    return steps


def chunks_of(steps):
    out = []
    for _, _, _, width in steps:
        n = width // P
        out.append([(b, min(4, n - b)) for b in range(0, n, 4)])
    if sum(map(len, out)) % 2:
        out[0] = [(b, min(2, 3 - b)) for b in range(0, 3, 2)]
    return out


def chunk_starts(chunks):
    starts = [0]
    for c in chunks:
        starts.append(starts[-1] + len(c))
    assert starts[-1] % 2 == 0
    return starts


LAST_PASS = dict(dsa=W_OUT1, fox=W_OUT2, dil=W_OUT3 + PLE_EXTRA)
PASSES = dict(dsa=3, fox=8, dil=8)
MIXER = dict(dsa=0, fox=1, dil=2)
ORDER = dict(dsa="TTNT", fox="TTNT", dil="TTTTTTNNNT")


def proj_units(kind, t):
    if kind != "dil":
        return [(t // 4, (t // 2) % 2, t % 2)], []
    first, last = (20 * t) // NT, (20 * (t + 1)) // NT
    units = [(h // 2, h % 2, None) for h in range(first, last)]
    return units[:1], units[1:]


def pass_beside(n):
    return 11 + n // 2 if n < 6 else 14 + (n - NT) // 2 if n >= NT else None


def value_cols(head):
    at, lo, out = head * DV, 0, []
    while lo < DV:
        w = min(DV - lo, P - (at + lo) % P)
        out.append((lo, (at + lo) // P, (at + lo) % P, w))
        lo += w
    return out


def mask_offset(i):
    return P * (i * (i + 1) // 2)


def host_constants():
    q = np.arange(P)[:, None]
    out = {}
    out["c_ident"] = np.eye(P, dtype=np.float32)
    out["c_flip"] = np.eye(P, dtype=np.float32)[::-1].copy()
    out["c_ones"] = np.ones((P, P), np.float32)
    out["c_diag"] = np.where(q >= np.arange(P)[None, :], 0.0, NEG).astype(np.float32)
    cols = []
    for (window, dil), nb in zip(DIL_PATTERN, DIL_NB):
        dist = q + (nb - 1) * P - np.arange(nb * P)[None, :]
        ok = (dist >= 0) & (dist <= window) & (dist % dil == 0)
        cols.append(np.where(ok, dist, 1e30).astype(np.float32))
    out["c_dist"] = np.concatenate(cols, axis=1)
    out["c_slope"] = np.broadcast_to(-(2.0 ** (-8.0 * np.arange(1, 25) / 24.0)), (P, 24)).astype(np.float32).copy()
    rel = np.maximum(255 - np.arange(384), 0)
    relf = np.maximum(rel, 1).astype(np.float32)
    large = 16 + (np.log(relf / np.float32(16)) / np.float32(math.log(8.0)) * np.float32(16)).astype(np.int32)
    bucket = np.where(rel < 16, rel, np.minimum(large, 31))
    out["c_bucket"] = (np.arange(32)[:, None] == bucket[None, :]).astype(np.float32)
    j = np.arange(P)[:, None]
    i = np.arange(P)[None, :]
    out["c_chunk"] = ((j // CH == i // CH) & (j <= i)).astype(np.int32)
    out["c_keep"] = np.broadcast_to((np.arange(T) % CH != 0), (P, T)).astype(np.float32).copy()
    cnt = np.zeros((2, P, T), np.float32)
    for g, w in enumerate((2, 4, 8, 16)):
        cnt[g // 2, (g % 2) * 64:(g % 2) * 64 + 64, :] = 1.0 / np.minimum(np.arange(T) + 1, w)
    out["c_cnt"] = cnt
    return out


def build(nc, a, stop=99):
    ctx = ExitStack()
    with ctx:
        def sb(name, shape, dt=F32):
            return ctx.enter_context(nc.sbuf_tensor(name, shape, dt))

        def ps(name, shape):
            return ctx.enter_context(nc.psum_tensor(name, shape, F32))

        def sem(name):
            return ctx.enter_context(nc.semaphore(name))

        hT = sb("hT", [P, KB, T])
        act_hi = sb("act_hi", [P, KB, T], F32R)
        act_lo = sb("act_lo", [P, KB, T], F32R)
        w_raw = sb("w_raw", [P, 2, KB, P])
        w_hi = sb("w_hi", [P, 2, KB, P], F32R)
        w_lo = sb("w_lo", [P, 2, KB, P], F32R)
        ident = sb("ident", [P, P])
        ones = sb("ones", [P, P])
        diag = sb("diag", [P, P])
        gains = sb("gains", [P, 5, KB])
        epsc = sb("epsc", [P, 1])
        A_COLS = 21900
        arena = sb("arena", [P, A_COLS])

        proj = [ps("proj0", [P, 512]), ps("proj1", [P, 512])]
        score = ps("score", [P, 2, 1024])
        obanks = [ps("out0", [P, 512]), ps("out1", [P, 512])]
        obank = obanks[0]

        yd = nc.dram_tensor("y_scratch", [D, T], F32).ap()
        xd = nc.dram_tensor("x_scratch", [P, KB, T], F32).ap()
        cd = nc.dram_tensor("decay_scratch", [16, T], F32).ap()
        rd = nc.dram_tensor("bias_scratch", [6, 384], F32).ap()

        class Area:
            def __init__(self, tensor, at=0, end=A_COLS):
                self.t, self.at, self.end = tensor, at, end

            def take(self, n):
                r = self.t[:, self.at:self.at + n]
                self.at += n
                assert self.at <= self.end, (self.at, self.end)
                return r

        w_loaded = [sem("w_loaded0"), sem("w_loaded1")]
        w_hi_done = sem("w_hi_done")
        w_split = sem("w_split")
        pass_done = [sem("pass_done0"), sem("pass_done1")]
        pass_free = [sem("pass_free0"), sem("pass_free1")]
        consts = sem("consts")
        eps_set = sem("eps_set")
        phase_end = sem("phase_end")

        def wait(eng, s, v):
            if isinstance(v, int) and v <= 0:
                return
            eng.wait_ge(s, v)

        def wait_pass(eng, s, p, per, local):
            if isinstance(p, int) and p * per + local <= 0:
                return
            eng.wait_ge(s, p * per + local)

        def passes(eng, kind, one):
            n = 3 if kind == "dsa" else 8
            one(0, 0, True)
            if n > 3:
                with eng.Fori(0, (n - 2) // 2) as it:
                    for u in (1, 2):
                        one(it * 2 + u, u % 2, True)
            else:
                one(1, 1, True)
            one(n - 1, (n - 1) % 2, False)

        def barrier(eng, k, stay=True):
            eng.drain().then_inc(phase_end, 1)
            if stay:
                eng.wait_ge(phase_end, 3 * k)

        def wview(ap):
            return ap.rearrange("(k p) c -> p k c", p=P)

        w_in = wview(a["w_in"][0])
        w_out = [wview(a["w_out"][0]), wview(a["fox_w_out_2"][0]), wview(a["dil_w_out_2"][0])]
        w_fox = wview(a["fox_w_in_2"][0])
        w_dil = wview(a["dil_w_in_2"][0])
        w_gate = [wview(a["ple_w_gate_2"][m]) for m in range(2)]
        w_up = [wview(a["ple_w_up_2"][m]) for m in range(2)]
        NCONST = 3 + 5

        h_flat = hT[:, :, :].rearrange("p k t -> p (k t)")
        F = Area(h_flat, 0, KB * T)
        gq = F.take(2 * T).rearrange("p (g t) -> p g t", g=2)
        gk = F.take(2 * T).rearrange("p (g t) -> p g t", g=2)
        gv = F.take(3 * T).rearrange("p (b t c) -> p b t c", b=3, c=P)
        amask = F.take(P).bitcast(I32)
        intra = F.take(4 * P).rearrange("p (n c) -> p n c", n=4)
        G = Area(arena)
        maskb = G.take(mask_offset(NT) // 2).bitcast(BF16)
        tbias = G.take(6 * 256).rearrange("p (h c) -> p h c", h=6)
        rb31 = G.take(6)
        wi_s = G.take(4 * NT).rearrange("p (t h) -> p t h", h=4)
        gw2 = G.take(2 * P).rearrange("p (g c) -> p g c", g=2)
        gb = G.take(2)
        gnorm = G.take(DV)
        pscale = G.take(2)
        pw = G.take(2 * P).rearrange("p (g c) -> p g c", g=2)
        state = G.take(2 * 192).rearrange("p (g c) -> p g c", g=2)
        gzT = G.take(T)
        gg = G.take(3 * T).rearrange("p (b t) -> p b t", b=3)
        at_idx = G.at
        qiT, kiT = G.take(T), G.take(T)
        rel_s = G.take(2 * T).rearrange("p (n t) -> p n t", n=2)
        work = G.take(T)
        top8 = G.take(8)
        at_tmp = G.at
        G2 = G
        gb_x = G2.take(2 * T).rearrange("p (g t) -> p g t", g=2)
        gb_e = G2.take(2 * T).rearrange("p (g t) -> p g t", g=2)
        g_o = G2.take(3 * T).rearrange("p (t c) -> p t c", c=GH * DV)
        kdN = G2.take(2 * P).rearrange("p (n c) -> p n c", n=2)
        g_ms = G2.take(2 * GH * NT)
        dec = G2.take(2 * NT * 2).rearrange("p (g c) -> p g c", g=2)
        G4 = Area(arena, at_idx)
        pu = G4.take(2 * T).rearrange("p (b t) -> p b t", b=2)
        pg = G4.take(2 * T).rearrange("p (b t) -> p b t", b=2)
        G3 = Area(arena, at_tmp)
        pa, pb = (G3.take(2 * T).rearrange("p (b t) -> p b t", b=2) for _ in range(2))
        pcnt = G3.take(2 * T).rearrange("p (b t) -> p b t", b=2)

        def projected(areas, groups):
            def take(n=T):
                return (areas[0] if areas[0].at + n <= areas[0].end else areas[1]).take(n)
            r = {"q": [take() for _ in range(groups)], "k": [take() for _ in range(groups)]}
            r["v"] = [take().rearrange("p (t c) -> p t c", c=P) for _ in range(groups)]
            r["g"] = take()
            return r

        def attention_area(area, width):
            return {"e": area.take(T), "p": [area.take(width) for _ in range(2)],
                    "pT": area.take(1024).rearrange("p (n c) -> p n c", n=2),
                    "o": area.take(256).rearrange("p (n c) -> p n c", n=2), "y": area.take(T), "st": area.take(3 * 16)}

        DS = Area(arena, mask_offset(NT) // 2 + 6 * 256 + 6)
        FX = Area(arena)
        cB = [[FX.take(T) for _ in range(2)] for _ in range(2)]
        ccol = FX.take(16 * NT).rearrange("p (t h) -> p t h", h=16)
        crow = FX.take(T)
        ctmp = FX.take(T)
        fb = FX.take(1)
        DL = Area(arena)
        cdist = DL.take(sum(DIL_NB) * P)
        cslope = DL.take(24)
        fields = dict(dsa=attention_area(DS, T), fox=attention_area(FX, T), dil=attention_area(DL, sum(DIL_NB) * P))
        DH = Area(h_flat, 0, KB * T)
        sets = dict(dsa=[projected([DS], 1) for _ in range(2)], fox=[projected([FX], 1) for _ in range(2)],
                    dil=[projected([DH, DL], 3) for _ in range(2)])
        N = Area(arena)
        nsq = [N.take(T) for _ in range(2)]
        nacc = N.take(T)
        ntmp = [N.take(T) for _ in range(2)]
        Y = Area(arena)
        Y.take(5 * T)
        xnat = Y.take(2 * T).rearrange("p (n c) -> p n c", n=2)
        U = Area(arena)
        upT = U.take(KB * T).rearrange("p (k t) -> p k t", k=KB)
        pnat = U.take(NT * 256).rearrange("p (t c) -> p t c", c=256)
        ple_e = [U.take(512) for _ in range(2)]
        ple_t = [U.take(512) for _ in range(2)]

        def sems(prefix, names):
            return {n: sem(f"{prefix}_{n}") for n in names.split()}

        X = sems("x", "in0 in1 tr out ev sent0 sent1")
        NORM = sems("norm", "sq acc sum root rstd scaled hi lo")
        NORM_EVENTS = dict(sq=KB, acc=KB - 1, sum=1, root=1, rstd=1, scaled=KB, hi=KB, lo=KB)
        NORM_TO_PARTS = (True, False, True, True, False)
        SPLIT = sems("act_split", "in hi lo")
        S_Y1, S_Y2, S_PLE0, S_Y3, S_PLE1 = range(5)

        def norm_wait(eng, m, what, v):
            if v > 0:
                before = sum(NORM_TO_PARTS[:m]) if what in ("hi", "lo") else m
                eng.wait_ge(NORM[what], before * NORM_EVENTS[what] + v)

        IX = sems("idx", "sc scfree relu acc top sel bias biast biasd flip")
        GL = sems("gla", "in win keep last diff mmul logit x lsig cum eb q k kdexp kd kdt kdn a am s0 u su o oe "
                         "sq ms root rstd on ot gate y ysent pool pmm py psent z")
        PL = [sems(f"ple{m}", "in tr ev r h") for m in range(2)]
        AT = {k: sems(k, "gate sdone sread pre mx edone rden tdone te pv oev ot y ysent")
              for k in ("dsa", "fox", "dil")}
        FC = sems("foxc", "x lsig cum sent t ev")
        xsent = sem("xsent")
        xback = sem("xback")
        windows = sem("pool_windows")
        decay_in = [sem("decay_in0"), sem("decay_in1")]
        dil_in = sem("dil_constants")

        block = ctx.enter_context(nc.Block())

        @block.sync
        def _(sp):
            def load(n, src, slot, cols=None):
                wait(sp, w_split, n - 1)
                dst = w_raw[:, slot]
                if cols is not None:
                    dst = dst[:, :, cols[0]:cols[1]]
                return sp.dma_start(dst, src)

            def whole(n, src, slot):
                load(n, src, slot).then_inc(w_loaded[slot], 16)

            def col(w, c):
                return w[:, :, c:c + P] if isinstance(c, int) else w[:, :, bass.ds(c, P)]

            n = 0
            whole(0, col(w_in, C_QI), 0)
            for r in range(4):
                load(1, w_in[:, :, C_KI:C_KI + 32], 1, (32 * r, 32 * r + 32)).then_inc(w_loaded[1], 16)
            load(2, w_in[:, :, C_WI:C_WI + 4], 0, (0, 4)).then_inc(w_loaded[0], 16)
            n = 3
            for base in (C_GQ, C_GK):
                for g in range(2):
                    for u in range(2):
                        c = base + (2 * g + u) * DK
                        load(n, w_in[:, :, c:c + DK], n % 2, (64 * u, 64 * u + DK)).then_inc(w_loaded[n % 2], 16)
                    n += 1
            for b in range(3):
                whole(n, col(w_in, C_GV + b * P), n % 2)
                n += 1
            load(n, w_in[:, :, C_GZ:C_GZ + 16], n % 2, (0, 16)).then_inc(w_loaded[n % 2], 16)
            n += 1
            for b in range(3):
                whole(n, col(w_in, C_GG + b * P), n % 2)
                n += 1
            for c in (C_PU, C_PU + P, C_PG, C_PG + P):
                whole(n, col(w_in, c), n % 2)
                n += 1
            assert n == N_FIRST
            with sp.Fori(0, 3) as it:
                for b, c in enumerate((C_DQ, C_DK, C_DV, C_DG)):
                    whole(W_DSA + b + it * 4, col(w_in, it * P + c), (W_DSA + b) % 2)

            def out_blocks(w, base):
                with sp.Fori(0, 4) as it:
                    for b in range(2):
                        whole(it * 2 + (base + b), col(w, it * (2 * P) + b * P), (base + b) % 2)

            def ple_blocks(m, base):
                for b in range(2):
                    wait(sp, w_split, base + b - 1)
                    dst = w_raw[:, (base + b) % 2].rearrange("p k c -> p (k c)").rearrange("p (k c) -> p k c", k=2)
                    sp.dma_start(dst, w_up[m][:, :, b * 512:(b + 1) * 512]).then_inc(w_loaded[(base + b) % 2], 16)
                out_blocks(w_gate[m], base + 2)

            if stop > 0:
                out_blocks(w_out[0], W_OUT1)
            if stop > 1:
                n = W_FOXF
                load(n, w_fox[:, :, 4 * D:4 * D + 16], n % 2, (0, 16)).then_inc(w_loaded[n % 2], 16)
                with sp.Fori(0, 8) as it:
                    for b in range(4):
                        whole(it * 4 + (W_FOX + b), col(w_fox, it * P + b * D), (W_FOX + b) % 2)
                out_blocks(w_out[1], W_OUT2)
                ple_blocks(0, W_PLE0)
            if stop > 2:
                with sp.Fori(0, 8) as it:
                    for b in range(10):
                        whole(it * 10 + (W_DIL + b), col(w_dil, it * P + b * D), (W_DIL + b) % 2)
                out_blocks(w_out[2], W_OUT3)
                ple_blocks(1, W_PLE1)

        w_total = {0: W_OUT1, 1: W_FOXF, 2: W_DIL}.get(stop, W_ALL)
        pieces = [1] * W_ALL
        pieces[1] = 4
        for n in range(3, 7):
            pieces[n] = 2

        def landed(n):
            return 16 * sum(pieces[m] for m in range(n % 2, n + 1, 2))

        @block.gpsimd
        def _(pool):
            def split(n, count, slot, passes):
                pool.wait_ge(w_loaded[slot], count)
                wait(pool, pass_done[1], passes)
                pool.tensor_tensor(w_hi[:, slot], w_raw[:, slot], ones[:, :].unsqueeze(1).broadcast_to([P, KB, P]),
                                   ALU.mult).then_inc(w_hi_done, 1)
                pool.wait_ge(w_hi_done, n + 1)
                pool.tensor_tensor(w_lo[:, slot], w_raw[:, slot], w_hi[:, slot].bitcast(F32),
                                   ALU.subtract).then_inc(w_split, 1)

            def passes_before(n):
                m = n - 2
                ends = m + 1
                for up in (W_PLE0, W_PLE1):
                    ends += 3 * min(max(m - up + 1, 0), 2)
                return ends

            def stretch(n0, n1):
                if n1 - n0 >= 2:
                    with pool.Fori(0, (n1 - n0) // 2) as it:
                        for b in range(2):
                            n = n0 + b
                            split(it * 2 + n, it * 16 + landed(n), n % 2, it * 2 + passes_before(n))
                if (n1 - n0) % 2:
                    split(n1 - 1, landed(n1 - 1), (n1 - 1) % 2, passes_before(n1 - 1))

            pool.wait_ge(consts, 16 * NCONST)
            for n in range(12):
                split(n, landed(n), n % 2, passes_before(n))
            edges = [12]
            for up in (W_PLE0, W_PLE1):
                if w_total > up + 2:
                    stretch(edges[-1], up + 2)
                    for n in (up + 2, up + 3):
                        split(n, landed(n), n % 2, passes_before(n))
                    edges.append(up + 4)
            stretch(edges[-1], w_total)

        @block.tensor
        def _(pe):
            def half_T(n, c, slot, half, part=None, up=None, fresh=None, bank=None):
                kk = KB if up is None else 2
                ks = range(kk) if part is None else range(part * kk // 2, (part + 1) * kk // 2)
                if ks[0] == 0:
                    if half == 0:
                        pe.wait_ge(w_split, n + 1)
                    wait(pe, pass_free[half], c)
                tok = slice(half * 512, half * 512 + 512)
                for k in ks:
                    if fresh is not None:
                        pe.wait_ge(fresh[0], fresh[1] + k + 1)
                    if up is None:
                        hi, lo = w_hi[:, slot, k], w_lo[:, slot, k]
                    else:
                        hi, lo = (w[:, slot].rearrange("p k c -> p (k c)")[:, k * 512 + up * P:k * 512 + up * P + P]
                                  for w in (w_hi, w_lo))
                    pe.matmul((proj[half] if bank is None else bank)[:, :], hi, act_hi[:, k, tok], start=(k == 0), stop=False)
                    pe.matmul((proj[half] if bank is None else bank)[:, :], hi, act_lo[:, k, tok], start=False, stop=False)
                    mm = pe.matmul((proj[half] if bank is None else bank)[:, :], lo, act_hi[:, k, tok], start=False, stop=(k == kk - 1))
                if ks[-1] == kk - 1:
                    mm.then_inc(pass_done[half], 1)

            def half_N(n, c, slot, half, part=None, width=P):
                ts = range(4) if part is None else range(part * 2, part * 2 + 2)
                if ts[0] == 0:
                    if half == 0:
                        pe.wait_ge(w_split, n + 1)
                    wait(pe, pass_free[half], c)
                for t in ts:
                    tok = slice((half * 4 + t) * P, (half * 4 + t + 1) * P)
                    out = proj[half][:, t * width:(t + 1) * width]
                    for k in range(KB):
                        hi, lo = w_hi[:, slot, k, 0:width], w_lo[:, slot, k, 0:width]
                        pe.matmul(out, act_hi[:, k, tok], hi, start=(k == 0), stop=False)
                        pe.matmul(out, act_hi[:, k, tok], lo, start=False, stop=False)
                        mm = pe.matmul(out, act_lo[:, k, tok], hi, start=False, stop=(k == KB - 1))
                if ts[-1] == 3:
                    mm.then_inc(pass_done[half], 1)

            def pass_T(n, c, slot, up=None, fresh=None):
                for half in range(2):
                    half_T(n, c, slot, half, up=up, fresh=fresh if half == 0 else None)

            def pass_N(n, c, slot, width=P):
                for half in range(2):
                    half_N(n, c, slot, half, width=width)

            def norm_sum(m):
                norm_wait(pe, m, "acc", KB - 1)
                for half in range(2):
                    mm = pe.matmul(score[:, 0, half * 512:half * 512 + 512], ones[:, :],
                                   nacc[:, half * 512:half * 512 + 512], start=True, stop=True)
                mm.then_inc(NORM["sum"], 1)

            pe.wait_ge(consts, 16 * NCONST)
            for t in range(NT):
                pe.wait_ge(X[f"in{t % 2}"], 16 * (t // 2 + 1))
                if t >= 2:
                    pe.wait_ge(X["ev"], t - 1)
                for k in range(KB):
                    mm = pe.transpose(score[:, t % 2, k * P:(k + 1) * P], xnat[:, t % 2, k * P:(k + 1) * P], ident[:, :])
                mm.then_inc(X["tr"], 1)
            barrier(pe, 1)
            norm_sum(0)
            barrier(pe, 2, stay=False)

            pass_T(0, 0, 0, fresh=(NORM["lo"], 0))
            pass_T(1, 1, 1)
            pass_N(2, 2, 0, width=4)
            pe.wait_ge(pass_free[0], 2)
            pe.wait_ge(pass_free[1], 2)
            count = 0

            def idx_scores(i):
                n = (i - 2) * IDX_H
                for h in range(IDX_H):
                    wait(pe, IX["relu"], n + h - 1)
                    for c in range(0, (i + 1) * P, 512):
                        w = min(512, (i + 1) * P - c)
                        mm = pe.matmul(score[:, h % 2, c:c + w], qiT[32 * h:32 * h + 32, i * P:(i + 1) * P],
                                       kiT[32 * h:32 * h + 32, c:c + w], start=True, stop=True,
                                       tile_position=(32 * h, 0))
                    mm.then_inc(IX["sc"], 1)

            pe.wait_ge(IX["bias"], 48)
            pe.matmul(obank[0:6, 0:384], gzT[0:32, 384:390], gzT[0:32, 0:384], start=True, stop=True).then_inc(IX["biast"], 1)
            pe.wait_ge(IX["biasd"], 16 * 7)
            for h in range(6):
                wait(pe, IX["flip"], h + 1)
                mm = pe.matmul(obank[:, 0:256], rel_s[:, 0, 0:P], work[:, 0:256] if h == 0 else
                               (rel_s[:, 0, P * 2:P * 4] if h == 1 else
                                rel_s[:, 0, P * 4:P * 6] if h == 2 else
                                rel_s[:, 0, P * 6:P * 8] if h == 3 else
                                rel_s[:, 1, 0:P * 2] if h == 4 else rel_s[:, 1, P * 2:P * 4]), start=True, stop=True)
                mm.then_inc(IX["biast"], 1)
            pe.wait_ge(IX["flip"], 7)
            def gla_logits():
                for half in range(2):
                    pe.wait_ge(pass_free[half], 11)
                pe.wait_ge(IX["relu"], 4 * IDX_H)
                pe.wait_ge(GL["win"], 16 * 8)
                for g in range(2):
                    for half in range(2):
                        mm = pe.matmul(score[:, g, half * 512:half * 512 + 512], gw2[0:16, g],
                                       gzT[0:16, half * 512:half * 512 + 512], start=True, stop=True)
                mm.then_inc(GL["logit"], 1)

            def beside_pass(n):
                c = pass_beside(n)
                return c, c, c % 2, n % 2

            def gla_step(n):
                t, g = n // 2, n % 2
                tok = slice(t * P, (t + 1) * P)
                wait(pe, GL["kdn"], n)
                pe.transpose(proj[0][:, 0:P], gb_x[:, g, tok], ident[:, :]).then_inc(GL["kdt"], 1)
                wait(pe, GL["am"], 2 * n)
                for u in range(2):
                    if u:
                        pe.wait_ge(GL["a"], 2 * n + 1)
                    pe.matmul(proj[1][:, u * P:(u + 1) * P], gk[64 * u:64 * u + DK, g, tok],
                              gq[64 * u:64 * u + DK, g, tok], start=True, stop=True).then_inc(GL["a"], 1)
                wait(pe, GL["oe"], n)
                for c in range(2):
                    ctok = slice(t * P + c * CH, t * P + (c + 1) * CH)
                    rows = slice(c * CH, (c + 1) * CH)
                    pe.wait_ge(GL["su"], 2 + 4 * n + 2 * c)
                    pe.matmul(obank[rows, 0:192], gq[:, g, ctok], state[:, g], start=True, stop=False,
                              skip_group_check=True)
                    pe.wait_ge(GL["kdn"], n + 1)
                    for hv in range(2):
                        for lo, b0, o0, w0 in value_cols(2 * g + hv):
                            mm = pe.matmul(obanks[1][:, hv * DV + lo:hv * DV + lo + w0], kdN[rows, n % 2],
                                           gv[rows, b0, t, o0:o0 + w0], start=True, stop=True)
                    mm.then_inc(GL["u"], 1)
                    if pass_beside(n):
                        half_T(*beside_pass(n), part=c, bank=score[:, 0, n % 2 * 512:n % 2 * 512 + 512])
                pe.wait_ge(GL["am"], 2 * n + 2)
                for hv in range(2):
                    for lo, b0, o0, w0 in value_cols(2 * g + hv):
                        mm = pe.matmul(obank[:, hv * DV + lo:hv * DV + lo + w0], intra[:, hv],
                                       gv[:, b0, t, o0:o0 + w0], start=False, stop=True, skip_group_check=True)
                mm.then_inc(GL["o"], 1)

            for i in range(2, NT):
                if i == 6:
                    pe.wait_ge(GL["x"], 2)
                if i == 7:
                    for half in range(2):
                        pe.wait_ge(pass_free[half], 14)
                idx_scores(i)
                for n in {2: (3, 4), 3: (5, 6), 4: (7, 8), 5: (9, 10)}.get(i, ()):
                    (pass_N if 7 <= n <= 9 else pass_T)(n, n, n % 2)
                if i == 5:
                    gla_logits()
                if i == 6:
                    for half in range(2):
                        pe.wait_ge(pass_free[half], 11)
                    pe.wait_ge(GL["k"], 2)
                if i >= 6:
                    pe.wait_ge(IX["relu"], IDX_H * (i - 1))
                    for n in range(8 * (i - 6), 8 * (i - 5)):
                        gla_step(n)
            barrier(pe, 3)

            pe.wait_ge(GL["on"], 2)
            for b in range(3):
                wait(pe, GL["y"], b)
                for t in range(NT):
                    mm = pe.transpose(score[:, b % 2, t * P:(t + 1) * P], g_o[:, t, b * P:(b + 1) * P], ident[:, :])
                mm.then_inc(GL["ot"], 1)
            for b in range(2):
                pe.wait_ge(GL["pool"], b + 1)
                pe.wait_ge(GL["y"], 3)
                for half in range(2):
                    mm = pe.matmul(score[:, b, half * 512:half * 512 + 512], pw[:, b],
                                   pa[:, b, half * 512:half * 512 + 512], start=True, stop=True)
                mm.then_inc(GL["pmm"], 1)
            barrier(pe, 4)

            def attention(kind, base, extra):
                S, R, order = AT[kind], fields[kind], ORDER[kind]
                steps = attention_steps(kind)
                chunks = chunks_of(steps)
                starts = chunk_starts(chunks)
                C, N, NB = starts[-1], len(steps), len(order)
                per = 1 if kind == "dil" else 2
                pieces = 2 if kind == "dil" else 1

                def project(p, units):
                    for b, half, part in units:
                        n = p * NB + (base + b)
                        (half_T if order[b] == "T" else half_N)(n, n + extra, (base + b) % 2, half, part)

                def one(p, turn_, follow):
                    Q = sets[kind][turn_]

                    def scores(s, piece):
                        i, hh, segs, _ = steps[s]
                        wait_pass(pe, S["sread"], p, N * pieces, s * pieces + piece)
                        for g, buf, c0, j0, nb, _ in segs:
                            if buf != piece:
                                continue
                            rows = slice(0, P) if kind == "dil" else slice(64 * hh, 64 * hh + 64)
                            c, end = c0, c0 + nb * P
                            while c < end:
                                w = min(512 - c % 512, end - c)
                                k0 = j0 * P + c - c0
                                mm = pe.matmul(score[:, 0, c:c + w], Q["q"][g][rows, i * P:(i + 1) * P],
                                               Q["k"][g][rows, k0:k0 + w], start=True, stop=True)
                                c += w
                        mm.then_inc(S["sdone"], 1)

                    def turn(s, p=p):
                        if (s + 1) % per == 0:
                            i = steps[s][0]
                            wait_pass(pe, S["oev"], p, N, s + 1)
                            pe.transpose(obanks[s % 2][:, 256:384], R["o"][:, i % 2], ident[:, :]).then_inc(S["ot"], 1)

                    def transposes(s, c):
                        if c >= len(chunks[s]):
                            return
                        q = starts[s] + c
                        b0, nb = chunks[s][c]
                        if c == 0:
                            wait_pass(pe, S["edone"], p, N, s + 1)
                        wait_pass(pe, S["te"], p, C, q - 1)
                        for b in range(nb):
                            mm = pe.transpose(score[:, 1, (q % 2) * 512 + b * P:(q % 2) * 512 + (b + 1) * P],
                                              R["p"][s % 2][:, (b0 + b) * P:(b0 + b + 1) * P], ident[:, :])
                        mm.then_inc(S["tdone"], 1)

                    def values(s, c):
                        if c >= len(chunks[s]):
                            return
                        i, hh, segs, _ = steps[s]
                        blocks = [(g, j0 + b) for g, _, _, j0, nb, _ in segs for b in range(nb)]
                        q = starts[s] + c
                        b0, nb = chunks[s][c]
                        wait_pass(pe, S["te"], p, C, q + 1)
                        if c == 0:
                            wait_pass(pe, S["oev"], p, N, s - 1)
                            if (s - 1) % per == 0:
                                wait_pass(pe, S["y"], p, NT, (s - 1) // per)
                        dh = P if kind == "dil" else 64
                        for b in range(nb):
                            g, j = blocks[b0 + b]
                            mm = pe.matmul(obanks[s % 2][:, 0:dh], R["pT"][:, q % 2, b * P:(b + 1) * P],
                                           Q["v"][g][:, j, hh * 64:hh * 64 + dh],
                                           start=(b0 + b == 0), stop=(b0 + b == len(blocks) - 1))
                        mm.then_inc(S["pv"], 1)

                    for half in range(2):
                        pe.wait_ge(pass_free[half], p * NB + (base + extra + NB - 1))
                    for piece in range(pieces):
                        scores(0, piece)
                    if not (isinstance(p, int) and p == 0):
                        turn(N - 2, p - 1)
                        turn(N - 1, p - 1)
                    scores(1, 0)
                    for t in range(N):
                        part1, part2 = proj_units(kind, t)
                        if t >= 2:
                            turn(t - 2)
                        transposes(t, 0)
                        transposes(t, 1)
                        if pieces == 2 and t + 1 < N:
                            scores(t + 1, 1)
                        if follow:
                            project(p + 1, part1)
                        if len(chunks[t]) > 2:
                            values(t, 0)
                            transposes(t, 2)
                            values(t, 1)
                            transposes(t, 3)
                        if follow:
                            project(p + 1, part2)
                        if t + 2 < N:
                            scores(t + 2, 0)
                        for c in range(0 if len(chunks[t]) <= 2 else 2, 4):
                            values(t, c)
                    if not follow:
                        turn(N - 2)
                        turn(N - 1)

                for t in range(N):
                    for units in proj_units(kind, t):
                        project(0, units)
                passes(pe, kind, one)

            def out_loop(base, extra, split):
                for b in range(2):
                    pass_T(base + b, base + b + extra, (base + b) % 2,
                           fresh=(SPLIT["lo"], KB * split) if b == 0 else None)
                with pe.Fori(0, 3) as it:
                    for b in range(2):
                        n = it * 2 + (base + 2 + b)
                        pass_T(n, n + extra, (base + b) % 2)

            def ple(m, base, extra, k):
                pe.wait_ge(PL[m]["in"], 16)
                for t in range(NT):
                    if t >= 2:
                        pe.wait_ge(PL[m]["ev"], t - 1)
                    for b in range(2):
                        mm = pe.transpose(score[:, t % 2, b * P:(b + 1) * P], pnat[:, t, b * P:(b + 1) * P], ident[:, :])
                    mm.then_inc(PL[m]["tr"], 1)
                pe.wait_ge(PL[m]["ev"], NT)
                for b in range(2):
                    for u in range(4):
                        pass_T(base + b, base + extra + 4 * b + u, (base + b) % 2, up=u)
                barrier(pe, k)
                out_loop(base + 2, extra + PLE_EXTRA, (S_PLE0, S_PLE1)[m])
                barrier(pe, k + 1)

            attention("dsa", W_DSA, 0)
            barrier(pe, 5)
            if stop > 0:
                out_loop(W_OUT1, 0, S_Y1)
                barrier(pe, 6)
            if stop > 1:
                norm_sum(1)
                barrier(pe, 7)
                norm_sum(2)
                barrier(pe, 8, stay=False)
                pass_T(W_FOXF, W_FOXF, W_FOXF % 2, fresh=(NORM["lo"], KB))
                pe.wait_ge(FC["cum"], 1)
                for t in range(NT):
                    mm = pe.transpose(obank[:, t * 16:t * 16 + 16], crow[0:16, t * P:(t + 1) * P], ident[0:16, 0:16])
                mm.then_inc(FC["t"], 1)
                pe.wait_ge(FC["ev"], 1)
                attention("fox", W_FOX, 0)
                barrier(pe, 9)
                out_loop(W_OUT2, 0, S_Y2)
                barrier(pe, 10)
                ple(0, W_PLE0, 0, 11)
            if stop > 2:
                norm_sum(3)
                barrier(pe, 13)
                attention("dil", W_DIL, PLE_EXTRA)
                barrier(pe, 14)
                out_loop(W_OUT3, PLE_EXTRA, S_Y3)
                barrier(pe, 15)
                ple(1, W_PLE1, PLE_EXTRA, 16)
                norm_sum(4)
                barrier(pe, 18)
            for t in range(NT):
                if t >= 2:
                    pe.wait_ge(X["out"], t - 1)
                for k in range(KB):
                    mm = pe.transpose(score[:, t % 2, k * P:(k + 1) * P], hT[:, k, t * P:(t + 1) * P], ident[:, :])
                mm.then_inc(X["tr"], 1)

        @block.scalar
        def _(act):
            def norm_act(m, into_parts):
                for k in range(KB):
                    norm_wait(act, m, "acc", k - 1)
                    act.activation(nsq[k % 2], hT[:, k], ACT.Square).then_inc(NORM["sq"], 1)
                norm_wait(act, m, "sum", 1)
                act.activation(nsq[0], score[:, 0], ACT.Sqrt, bias=epsc[:, 0:1], scale=1.0 / D).then_inc(NORM["root"], 1)
                if into_parts:
                    for k in range(KB):
                        norm_wait(act, m, "scaled", k + 1)
                        act.activation(act_hi[:, k], ntmp[k % 2], ACT.Copy).then_inc(NORM["hi"], 1)

            def split_act(src):
                for k in range(KB):
                    act.activation(act_hi[:, k], src[:, k], ACT.Copy).then_inc(SPLIT["hi"], 1)

            def evac(c, dst, scale=1.0, rows=slice(0, P), done=None, width=512):
                for half in range(2):
                    act.wait_ge(pass_done[half], c + 1)
                    ins = act.activation(dst[rows, half * width:(half + 1) * width], proj[half][rows, 0:width],
                                         ACT.Copy, scale=scale)
                    ins.then_inc(pass_free[half], 1)

            act.dma_start(ident[:, :], a["c_ident"]).then_inc(consts, 16)
            act.dma_start(ones[:, :], a["c_ones"]).then_inc(consts, 16)
            act.dma_start(diag[:, :], a["c_diag"]).then_inc(consts, 16)
            for m, name in enumerate(("norm_g", "final_norm_g", "fox_norm_2", "dil_norm_2", "final_norm_2")):
                v = a[name] if len(a[name].shape) == 1 else a[name][0]
                act.dma_start(gains[:, m], v.rearrange("(k p) -> p k", p=P), allow_slow_non_contiguous=True).then_inc(consts, 16)
            for t in range(NT):
                if t >= 2:
                    act.wait_ge(X["tr"], t - 1)
                act.dma_start(xnat[:, t % 2], a["x"][0, t * P:(t + 1) * P, :]).then_inc(X[f"in{t % 2}"], 16)
                if t >= 1:
                    act.wait_ge(X["tr"], t)
                    act.activation(hT[:, :, (t - 1) * P:t * P], score[:, (t - 1) % 2].rearrange("p (k c) -> p k c", c=P),
                                   ACT.Copy).then_inc(X["ev"], 1)
            act.wait_ge(X["tr"], NT)
            act.activation(hT[:, :, (NT - 1) * P:], score[:, (NT - 1) % 2].rearrange("p (k c) -> p k c", c=P),
                           ACT.Copy).then_inc(X["ev"], 1)
            act.wait_ge(X["ev"], NT)
            act.dma_start(xd, hT[:, :, :]).then_inc(xsent, 16)
            act.wait_ge(consts, 16 * NCONST)
            act.wait_ge(eps_set, 1)
            barrier(act, 1)
            norm_act(0, True)
            act.wait_ge(xsent, 16)
            barrier(act, 2)

            act.dma_start(gzT[0:32, 0:384], a["c_bucket"]).then_inc(IX["bias"], 16)
            act.dma_start(gzT[0:32, 384:390], a["rel_bias"]).then_inc(IX["bias"], 16)
            act.dma_start(rel_s[:, 0, 0:P], a["c_flip"]).then_inc(IX["bias"], 16)
            act.dma_start(rb31, a["rel_bias"][31:32, :].broadcast_to([P, 6])).then_inc(GL["in"], 16)
            act.dma_start(gnorm, a["gla_norm_g"].broadcast_to([P, DV])).then_inc(GL["in"], 16)
            act.dma_start(pscale, a["pool_scale"][0].rearrange("(b p) -> p b", p=P), allow_slow_non_contiguous=True).then_inc(GL["in"], 16)
            act.dma_start(amask, a["c_chunk"]).then_inc(GL["in"], 16)
            act.wait_ge(GL["z"], 3)
            for half in range(2):
                act.dma_start(gw2[0:16, :, 64 * half:64 * half + DK],
                              a["gla_gate_w2"][0].rearrange("r (g u c) -> u r g c", u=2, c=DK)[half]).then_inc(GL["win"], 16)
                act.dma_start(gb[64 * half:64 * half + DK, :],
                              a["gla_gate_b"][0].rearrange("(g u c) -> u c g", u=2, c=DK)[half],
                              allow_slow_non_contiguous=True).then_inc(GL["win"], 16)
            for n in range(4):
                rows = slice(64 * (n % 2), 64 * (n % 2) + 64)
                act.dma_start(pw[rows, n // 2, rows], a["pool_w"][0, n]).then_inc(GL["win"], 16)
            act.dma_start(g_o.rearrange("p t c -> p (t c)")[:, 0:T], a["c_keep"]).then_inc(GL["keep"], 16)
            evac(0, qiT)
            evac(1, kiT)
            evac(2, wi_s.rearrange("p t h -> p (t h)"), scale=IDX_H ** -0.5, width=16)
            act.wait_ge(IX["biast"], 1)
            act.activation(work[0:6, 512:896], obank[0:6, 0:384], ACT.Copy).then_inc(IX["flip"], 1)
            act.wait_ge(IX["flip"], 1)
            act.dma_start(rd, work[0:6, 512:896]).then_inc(IX["biasd"], 16)
            act.wait_ge(IX["biasd"], 16)
            for h in range(6):
                dst = (work[:, 0:256], rel_s[:, 0, 256:512], rel_s[:, 0, 512:768], rel_s[:, 0, 768:1024],
                       rel_s[:, 1, 0:256], rel_s[:, 1, 256:512])[h]
                base = rd[h:h + 1, 0:256]
                src = bass.AP(tensor=base.tensor, offset=base.offset, ap=[[1, P], [1, 256]])
                act.dma_start(dst, src).then_inc(IX["biasd"], 16)
            act.wait_ge(GL["in"], 64)
            for h in range(6):
                act.wait_ge(IX["biast"], h + 2)
                act.activation(tbias[:, h], obank[:, 0:256], ACT.Copy).then_inc(IX["flip"], 1)

            def idx_relu(i):
                n = (i - 2) * IDX_H
                for h in range(IDX_H):
                    w = (i + 1) * P
                    act.wait_ge(IX["sc"], n + h + 1)
                    wait(act, IX["acc"], n + h - 1)
                    act.activation(rel_s[:, h % 2, 0:w], score[:, h % 2, 0:w], ACT.Relu,
                                   scale=IDX_D ** -0.5).then_inc(IX["relu"], 1)

            targets = {3: gq[:, 0], 4: gq[:, 1], 5: gk[:, 0], 6: gk[:, 1], 7: gv[:, 0].rearrange("p t c -> p (t c)"),
                       8: gv[:, 1].rearrange("p t c -> p (t c)"), 9: gv[:, 2].rearrange("p t c -> p (t c)"), 10: gzT,
                       11: gg[:, 0], 12: gg[:, 1], 13: gg[:, 2], 14: pu[:, 0], 15: pu[:, 1], 16: pg[:, 0], 17: pg[:, 1]}

            def gate_sums():
                act.wait_ge(GL["x"], 2)
                act.activation(gb_e, gb_x, ACT.Abs).then_inc(GL["lsig"], 1)
                act.wait_ge(GL["lsig"], 1)
                act.activation(gb_e, gb_e, ACT.Exp, scale=-1.0).then_inc(GL["lsig"], 1)
                act.wait_ge(GL["lsig"], 2)
                act.activation(gb_e, gb_e, ACT.Ln, bias=1.0).then_inc(GL["lsig"], 1)
                act.wait_ge(GL["cum"], 2)
                act.activation(gb_e, gb_x, ACT.Exp, scale=1.0 / 16).then_inc(GL["eb"], 1)
                act.wait_ge(GL["q"], 3)
                act.activation(gb_e, gb_x, ACT.Exp, scale=-1.0 / 16).then_inc(GL["eb"], 1)
                act.wait_ge(GL["diff"], 2)
                act.activation(gb_x, gb_x, ACT.Exp, scale=1.0 / 16).then_inc(GL["kdexp"], 1)

            def gla_step(n):
                act.wait_ge(GL["kdt"], n + 1)
                wait(act, GL["u"], 2 * (n - 1))
                act.activation(kdN[:, n % 2], proj[0][:, 0:P], ACT.Copy).then_inc(GL["kdn"], 1)
                act.wait_ge(GL["o"], n + 1)
                t, g = n // 2, n % 2
                act.activation(g_o[:, t, g * 192:(g + 1) * 192], obank[:, 0:192], ACT.Copy).then_inc(GL["oe"], 1)
                if pass_beside(n):
                    c, half = pass_beside(n), n % 2
                    act.wait_ge(pass_done[half], c + 1)
                    if n >= NT:
                        act.wait_ge(IX["acc"], IDX_H * (NT - 2))
                    act.activation(targets[c][:, half * 512:half * 512 + 512], score[:, 0, half * 512:half * 512 + 512],
                                   ACT.Copy).then_inc(pass_free[half], 1)

            for i in range(2, NT):
                idx_relu(i)
                for n in {2: (3, 4), 3: (5, 6), 4: (7, 8), 5: (9, 10)}.get(i, ()):
                    evac(n, targets[n], scale=DK ** -0.5 if n in (3, 4) else 1.0)
                if i == 5:
                    gate_sums()
                if i >= 6:
                    for n in range(8 * (i - 6), 8 * (i - 5)):
                        gla_step(n)
            barrier(act, 3)

            act.wait_ge(GL["ms"], 1)
            act.activation(g_ms[:, 0:32], g_ms[:, 0:32], ACT.Sqrt, bias=epsc[:, 0:1], scale=1.0 / DV).then_inc(GL["root"], 1)
            act.wait_ge(GL["on"], 2)
            for b in range(3):
                act.activation((gb_x[:, 0], gb_x[:, 1], gb_e[:, 0])[b], gg[:, b], ACT.Sigmoid).then_inc(GL["gate"], 1)
            for b in range(2):
                act.activation(gq[:, b], pg[:, b], ACT.Sigmoid).then_inc(GL["gate"], 1)
            for b in range(3):
                act.wait_ge(GL["y"], b + 1)
                act.dma_start(yd[b * P:(b + 1) * P, :], gg[:, b]).then_inc(GL["ysent"], 16)
            act.dma_start(pcnt, a["c_cnt"].rearrange("b p t -> p b t")).then_inc(GL["psent"], 16)
            for b in range(2):
                act.wait_ge(GL["py"], b + 1)
                act.dma_start(yd[(6 + b) * P:(7 + b) * P, :], pg[:, b]).then_inc(GL["ysent"], 16)
            act.wait_ge(GL["ysent"], 16 * 5)
            barrier(act, 4)

            def last_row(kind):
                return 5 if kind == "dsa" else KB - 1

            def load_y(kind):
                act.wait_ge(AT[kind]["ysent"], 16 * (PASSES[kind] - 1))
                for half in range(2):
                    act.wait_ge(pass_done[half], LAST_PASS[kind])
                for k in range(KB):
                    if k != last_row(kind):
                        act.dma_start(act_lo[:, k].bitcast(F32), yd[k * P:(k + 1) * P, :]).then_inc(SPLIT["in"], 16)

            def split_y(kind):
                k = last_row(kind)
                act.dma_start(act_lo[:, k].bitcast(F32), yd[k * P:(k + 1) * P, :]).then_inc(SPLIT["in"], 16)
                act.wait_ge(SPLIT["in"], 16 * KB * (MIXER[kind] + 1))
                split_act(act_lo[:, :, :].bitcast(F32))

            def attention(kind, base, extra, rows):
                S, R, order = AT[kind], fields[kind], ORDER[kind]
                steps = attention_steps(kind)
                chunks = chunks_of(steps)
                starts = chunk_starts(chunks)
                C, N, NB = starts[-1], len(steps), len(order)
                scale = 128 ** -0.5 if kind == "dil" else 0.125
                groups = 3 if kind == "dil" else 1

                def decay(p, turn_):
                    if kind == "fox":
                        for hh in range(2):
                            row = cd[2 * p + hh:2 * p + hh + 1, :] if isinstance(p, int) else cd[bass.ds(p * 2 + hh, 1), :]
                            act.dma_start(cB[turn_][hh], row.broadcast_to([P, T])).then_inc(decay_in[turn_], 16)

                def projected(p, turn_, units):
                    Q = sets[kind][turn_]
                    dsts = Q["q"] + Q["k"] + [v.rearrange("p t c -> p (t c)") for v in Q["v"]] + [Q["g"]]
                    for b, half, part in units:
                        if part == 0:
                            continue
                        act.wait_ge(pass_done[half], p * NB + (base + extra + b + 1))
                        act.activation(dsts[b][:, half * 512:half * 512 + 512], proj[half][:, :], ACT.Copy,
                                       scale=scale if b < groups else 1.0).then_inc(pass_free[half], 1)

                def store(p):
                    wait_pass(act, S["y"], p, NT, NT)
                    at = p * P + rows
                    act.dma_start(yd[at:at + P, :] if isinstance(p, int) else yd[bass.ds(at, P), :], R["y"])\
                       .then_inc(S["ysent"], 16)

                def one(p, turn_, follow):
                    Q = sets[kind][turn_]

                    def exp(s):
                        width = steps[s][3]
                        wait_pass(act, S["mx"], p, N, s + 1)
                        act.activation(R["p"][s % 2][:, 0:width], R["p"][s % 2][:, 0:width], ACT.Exp,
                                       bias=R["st"][:, s:s + 1], accum_out=R["st"][:, 16 + s:17 + s]).then_inc(S["edone"], 1)

                    def turned(s, c):
                        if c >= len(chunks[s]):
                            return
                        q, nb = starts[s] + c, chunks[s][c][1]
                        wait_pass(act, S["tdone"], p, C, q + 1)
                        wait_pass(act, S["pv"], p, C, q - 1)
                        act.activation(R["pT"][:, q % 2, 0:nb * P], score[:, 1, (q % 2) * 512:(q % 2) * 512 + nb * P],
                                       ACT.Copy).then_inc(S["te"], 1)

                    exp(0)
                    if not (isinstance(p, int) and p == 0):
                        store(p - 1)
                    if not follow:
                        load_y(kind)
                    for half in range(2):
                        act.wait_ge(pass_free[half], p * NB + (base + extra + NB))
                    if follow:
                        decay(p + 1, 1 - turn_)
                    act.activation(R["e"], Q["g"], ACT.Tanh, scale=0.5).then_inc(S["gate"], 1)
                    for t in range(N):
                        part1, part2 = proj_units(kind, t)
                        turned(t, 0)
                        turned(t, 1)
                        if follow and kind == "dil":
                            projected(p + 1, 1 - turn_, part1)
                        turned(t, 2)
                        turned(t, 3)
                        if t + 1 < N:
                            exp(t + 1)
                        if follow:
                            projected(p + 1, 1 - turn_, part2 if kind == "dil" else part1)
                    if not follow:
                        store(p)

                decay(0, 0)
                for t in range(N):
                    for units in proj_units(kind, t):
                        projected(0, 0, units)
                passes(act, kind, one)
                act.wait_ge(S["ysent"], 16 * PASSES[kind])

            def ple(m, base, extra, k):
                act.dma_start(pnat, a["p_2"][m, 0].rearrange("(t p) c -> p t c", p=P)).then_inc(PL[m]["in"], 16)
                for t in range(NT):
                    act.wait_ge(PL[m]["tr"], t + 1)
                    act.activation(act_hi[:, 0:2, t * P:(t + 1) * P],
                                   score[:, t % 2, 0:256].rearrange("p (b c) -> p b c", b=2), ACT.Copy).then_inc(PL[m]["h"], 1)
                for cb in range(8):
                    evac(base + extra + cb, upT[:, cb])
                barrier(act, k)
                split_act(hT)
                with act.Fori(0, 4) as it:
                    for b in range(2):
                        for half in range(2):
                            c = it * 2 + (base + 2 + extra + PLE_EXTRA + b)
                            act.wait_ge(pass_done[half], c + 1)
                            act.wait_ge(PL[m]["r"], it * 8 + (4 * b + 2 * half + 6))
                            act.activation(ple_e[half], proj[half][:, :], ACT.Sigmoid).then_inc(pass_free[half], 1)
                barrier(act, k + 1)

            attention("dsa", W_DSA, 0, 3 * P)
            act.dma_start(hT[:, :, :], xd).then_inc(xback, 16)
            act.wait_ge(xback, 16)
            barrier(act, 5)
            if stop > 0:
                split_y("dsa")
                barrier(act, 6)
            if stop > 1:
                norm_act(1, False)
                barrier(act, 7)
                norm_act(2, True)
                barrier(act, 8)
                act.dma_start(fb[0:16, 0:1], a["fox_b_f_2"][0].rearrange("(h o) -> h o", o=1), allow_slow_non_contiguous=True).then_inc(FC["x"], 16)
                evac(W_FOXF, crow, rows=slice(0, 16))
                act.wait_ge(FC["x"], 17)
                act.activation(ctmp[0:16], crow[0:16], ACT.Abs).then_inc(FC["lsig"], 1)
                act.wait_ge(FC["lsig"], 1)
                act.activation(ctmp[0:16], ctmp[0:16], ACT.Exp, scale=-1.0).then_inc(FC["lsig"], 1)
                act.wait_ge(FC["lsig"], 2)
                act.activation(ctmp[0:16], ctmp[0:16], ACT.Ln, bias=1.0).then_inc(FC["lsig"], 1)
                act.wait_ge(FC["cum"], 1)
                act.dma_start(cd, crow[0:16]).then_inc(FC["sent"], 16)
                act.wait_ge(FC["sent"], 16)
                attention("fox", W_FOX, 0, 0)
                barrier(act, 9)
                split_y("fox")
                barrier(act, 10)
                ple(0, W_PLE0, 0, 11)
            if stop > 2:
                act.dma_start(xd, hT[:, :, :]).then_inc(xsent, 16)
                norm_act(3, True)
                act.wait_ge(xsent, 32)
                barrier(act, 13)
                act.dma_start(cdist, a["c_dist"]).then_inc(dil_in, 16)
                act.dma_start(cslope, a["c_slope"]).then_inc(dil_in, 16)
                attention("dil", W_DIL, PLE_EXTRA, 0)
                act.dma_start(hT[:, :, :], xd).then_inc(xback, 16)
                act.wait_ge(xback, 32)
                barrier(act, 14)
                split_y("dil")
                barrier(act, 15)
                ple(1, W_PLE1, PLE_EXTRA, 16)
                norm_act(4, False)
                barrier(act, 18)
            for t in range(NT):
                act.wait_ge(X["tr"], NT + t + 1)
                if t >= 2:
                    act.wait_ge(X[f"sent{t % 2}"], 16 * (t // 2))
                act.activation(xnat[:, t % 2], score[:, t % 2], ACT.Copy).then_inc(X["out"], 1)
                act.wait_ge(X["out"], t + 1)
                act.dma_start(a["out"][0, t * P:(t + 1) * P, :], xnat[:, t % 2]).then_inc(X[f"sent{t % 2}"], 16)
            for slot in range(2):
                act.wait_ge(X[f"sent{slot}"], 16 * (NT // 2))

        @block.vector
        def _(dve):
            def norm_dve(m, into_parts):
                for k in range(1, KB):
                    norm_wait(dve, m, "sq", k + 1)
                    if k > 1:
                        norm_wait(dve, m, "acc", k - 1)
                    dve.tensor_tensor(nacc, nsq[0] if k == 1 else nacc, nsq[k % 2], ALU.add).then_inc(NORM["acc"], 1)
                norm_wait(dve, m, "root", 1)
                dve.reciprocal(nacc, nsq[0]).then_inc(NORM["rstd"], 1)
                norm_wait(dve, m, "rstd", 1)
                for k in range(KB):
                    if into_parts:
                        if k >= 2:
                            norm_wait(dve, m, "lo", k - 1)
                        dve.scalar_tensor_tensor(ntmp[k % 2], hT[:, k], gains[:, m, k:k + 1], nacc, ALU.mult, ALU.mult)\
                           .then_inc(NORM["scaled"], 1)
                        norm_wait(dve, m, "hi", k + 1)
                        dve.tensor_tensor(act_lo[:, k], ntmp[k % 2], act_hi[:, k].bitcast(F32), ALU.subtract)\
                           .then_inc(NORM["lo"], 1)
                    else:
                        dve.scalar_tensor_tensor(hT[:, k], hT[:, k], gains[:, m, k:k + 1], nacc, ALU.mult, ALU.mult)\
                           .then_inc(NORM["scaled"], 1)

            def split_dve(m, src):
                for k in range(KB):
                    dve.wait_ge(SPLIT["hi"], m * KB + k + 1)
                    dve.tensor_tensor(act_lo[:, k], src[:, k], act_hi[:, k].bitcast(F32), ALU.subtract)\
                       .then_inc(SPLIT["lo"], 1)

            dve.memset(epsc[:, :], EPS).then_inc(eps_set, 1)
            barrier(dve, 1)
            norm_dve(0, True)
            barrier(dve, 2)

            g = GL
            for pad in (gw2, gb, pw):
                dve.memset(pad, 0.0).then_inc(GL["z"], 1)
            dve.memset(state, 0.0).then_inc(g["su"], 1)
            dve.memset(intra, 0.0).then_inc(g["su"], 1)

            def gate_logits():
                for b in range(2):
                    dve.tensor_scalar(gb_x[:, b], score[:, b], gb[:, b:b + 1], None, ALU.add).then_inc(g["x"], 1)

            def gate_sums():
                dve.wait_ge(g["lsig"], 3)
                for b in range(2):
                    dve.scalar_tensor_tensor(gb_x[:, b], gb_x[:, b], 0.0, gb_e[:, b], ALU.min, ALU.subtract)\
                       .then_inc(g["lsig"], 1)
                dve.wait_ge(g["lsig"], 5)
                dve.wait_ge(g["keep"], 16)
                for b in range(2):
                    dve.tensor_tensor_scan(gb_x[:, b], g_o.rearrange("p t c -> p (t c)")[:, 0:T], gb_x[:, b], 0.0,
                                           ALU.mult, ALU.add).then_inc(g["cum"], 1)

            def decayed_queries():
                dve.wait_ge(g["eb"], 1)
                for b in range(2):
                    dve.tensor_tensor(gq[:, b], gq[:, b], gb_e[:, b], ALU.mult).then_inc(g["q"], 1)
                dve.tensor_copy(dec, gb_e.rearrange("p g (c j) -> p g c j", j=CH)[:, :, :, CH - 1]).then_inc(g["q"], 1)
                dve.wait_ge(g["cum"], 2)
                for b in range(2):
                    dve.tensor_copy(g_ms[:, b * 16:b * 16 + 16],
                                    gb_x[:, b].rearrange("p (c j) -> p c j", j=CH)[:, :, CH - 1]).then_inc(g["last"], 1)

            def to_chunk_end():
                dve.wait_ge(g["last"], 2)
                dve.wait_ge(g["eb"], 2)
                for b in range(2):
                    x3 = gb_x[:, b].rearrange("p (c j) -> p c j", j=CH)
                    dve.tensor_tensor(x3, g_ms[:, b * 16:b * 16 + 16].unsqueeze(2).broadcast_to([P, 16, CH]), x3,
                                      ALU.subtract).then_inc(g["diff"], 1)

            def decayed_keys():
                dve.wait_ge(g["kdexp"], 1)
                for b in range(2):
                    dve.tensor_tensor(gb_x[:, b], gb_x[:, b], gk[:, b], ALU.mult).then_inc(g["kd"], 1)
                dve.wait_ge(g["kd"], 2)
                for b in range(2):
                    dve.tensor_tensor(gk[:, b], gk[:, b], gb_e[:, b], ALU.mult).then_inc(g["k"], 1)

            def gla_chunk(n, c):
                t, b = n // 2, n % 2
                if c == 0:
                    for u in range(2):
                        dve.wait_ge(g["a"], 2 * n + 2)
                        wait(dve, g["o"], n)
                        dve.wait_ge(g["su"], 2)
                        dve.copy_predicated(intra[:, u], amask, proj[1][:, u * P:(u + 1) * P]).then_inc(g["am"], 1)
                dve.wait_ge(g["u"], 2 * n + c + 1)
                dve.wait_ge(g["su"], 2 + 4 * n + 2 * c)
                for u in range(2):
                    rows, cols = slice(64 * u, 64 * u + DK), slice(u * DV, (u + 1) * DV)
                    dve.scalar_tensor_tensor(state[rows, b, cols], state[rows, b, cols],
                                             dec[rows, b, 2 * t + c:2 * t + c + 1], obanks[1][rows, cols],
                                             ALU.mult, ALU.add).then_inc(g["su"], 1)

            def beside(i, r):
                if i == 5 and r in (7, 12, 18, 22, 26):
                    if r == 7:
                        dve.wait_ge(g["logit"], 1)
                    {7: gate_logits, 12: gate_sums, 18: decayed_queries, 22: to_chunk_end, 26: decayed_keys}[r]()
                if i >= 6 and r % 2:
                    j = 16 * (i - 6) + r // 2
                    gla_chunk(j // 2, j % 2)

            dve.wait_ge(pass_free[0], 3)
            dve.wait_ge(pass_free[1], 3)
            dve.wait_ge(IX["flip"], 7)
            dve.wait_ge(GL["in"], 64)
            for h in range(6):
                dve.tensor_scalar(tbias[:, h], tbias[:, h], rb31[:, h:h + 1], None, ALU.subtract).then_inc(IX["bias"], 1)
            sel = 0
            for i in range(2):
                if i:
                    dve.memset(maskb[:, mask_offset(i):mask_offset(i) + P * i], 0.0).then_inc(IX["sel"], 1)
                    sel += 1
                dve.tensor_copy(maskb[:, mask_offset(i) + P * i:mask_offset(i + 1)], diag[:, :]).then_inc(IX["sel"], 1)
                sel += 1
            top = 0
            for i in range(2, NT):
                n = (i - 2) * IDX_H
                w = (i + 1) * P
                for h in range(IDX_H):
                    dve.wait_ge(IX["relu"], n + h + 1)
                    if h == 0:
                        wait(dve, IX["sel"], sel)
                        dve.tensor_scalar(work[:, 0:w], rel_s[:, 0, 0:w], wi_s[:, i, 0:1], None, ALU.mult)\
                           .then_inc(IX["acc"], 1)
                    else:
                        dve.wait_ge(IX["acc"], n + h)
                        dve.scalar_tensor_tensor(work[:, 0:w], rel_s[:, h % 2, 0:w], wi_s[:, i, h:h + 1], work[:, 0:w],
                                                 ALU.mult, ALU.add).then_inc(IX["acc"], 1)
                dve.wait_ge(IX["acc"], n + IDX_H)
                dve.tensor_tensor(work[:, i * P:w], work[:, i * P:w], diag[:, :], ALU.add).then_inc(IX["top"], 1)
                top += 1
                for r in range(TOPK // 8):
                    dve.wait_ge(IX["top"], top)
                    dve.max(top8, work[:, 0:w]).then_inc(IX["top"], 1)
                    dve.wait_ge(IX["top"], top + 1)
                    dve.match_replace(work[:, 0:w], top8, work[:, 0:w], -3e38).then_inc(IX["top"], 1)
                    top += 2
                    beside(i, r)
                dve.wait_ge(IX["top"], top)
                dve.tensor_scalar(maskb[:, mask_offset(i):mask_offset(i + 1)], work[:, 0:w], -2e38, NEG,
                                  ALU.is_gt, ALU.mult).then_inc(IX["sel"], 1)
                sel += 1
            barrier(dve, 3)

            dve.wait_ge(g["oe"], 2 * NT)
            o_flat = g_o.rearrange("p t c -> p (t c)")
            o3 = o_flat.rearrange("p (n v) -> p n v", v=DV)
            sq = arena[:, at_tmp:at_tmp + 3 * T]
            dve.tensor_tensor(sq, o_flat, o_flat, ALU.mult).then_inc(g["sq"], 1)
            dve.wait_ge(g["sq"], 1)
            dve.tensor_reduce(g_ms[:, 0:32], sq.rearrange("p (n v) -> p n v", v=DV), AX.X, ALU.add).then_inc(g["ms"], 1)
            dve.wait_ge(g["root"], 1)
            dve.reciprocal(g_ms[:, 32:64], g_ms[:, 0:32]).then_inc(g["rstd"], 1)
            dve.wait_ge(g["rstd"], 1)
            dve.tensor_tensor(o3, o3, g_ms[:, 32:64].unsqueeze(2).broadcast_to([P, 32, DV]), ALU.mult).then_inc(g["on"], 1)
            dve.wait_ge(g["on"], 1)
            dve.tensor_tensor(o3, o3, gnorm.unsqueeze(1).broadcast_to([P, 32, DV]), ALU.mult).then_inc(g["on"], 1)
            es = [gb_x[:, 0], gb_x[:, 1], gb_e[:, 0], gq[:, 0], gq[:, 1]]
            zs = [gg[:, 0], gg[:, 1], gg[:, 2], pg[:, 0], pg[:, 1]]
            for n in range(5):
                dve.wait_ge(g["gate"], n + 1)
                dve.tensor_tensor(zs[n], zs[n], es[n], ALU.mult).then_inc(g["mmul"], 1)
            for b in range(3):
                dve.wait_ge(g["ot"], b + 1)
                dve.wait_ge(g["mmul"], b + 1)
                dve.tensor_tensor(gg[:, b], score[:, b % 2], gg[:, b], ALU.mult).then_inc(g["y"], 1)

            dve.wait_ge(g["mmul"], 5)
            dve.wait_ge(g["y"], 3)
            dve.tensor_copy(pa[:, :, 0:1], pu[:, :, 0:1]).then_inc(windows, 1)
            dve.tensor_tensor(pa[:, :, 1:T], pu[:, :, 1:T], pu[:, :, 0:T - 1], ALU.add).then_inc(windows, 1)
            dve.wait_ge(windows, 2)
            dve.tensor_copy(pb[:, :, 0:2], pa[:, :, 0:2]).then_inc(windows, 1)
            dve.tensor_tensor(pb[:, :, 2:T], pa[:, :, 2:T], pa[:, :, 0:T - 2], ALU.add).then_inc(windows, 1)
            dve.wait_ge(windows, 4)
            dve.tensor_copy(pa[:, 1, 0:4], pb[:, 1, 0:4]).then_inc(windows, 1)
            dve.tensor_tensor(pa[:, 1, 4:T], pb[:, 1, 4:T], pb[:, 1, 0:T - 4], ALU.add).then_inc(windows, 1)
            dve.wait_ge(windows, 6)
            dve.tensor_copy(pb[64:P, 1, 0:8], pa[64:P, 1, 0:8]).then_inc(windows, 1)
            dve.tensor_tensor(pb[64:P, 1, 8:T], pa[64:P, 1, 8:T], pa[64:P, 1, 0:T - 8], ALU.add).then_inc(windows, 1)
            dve.wait_ge(g["psent"], 16)
            dve.wait_ge(windows, 8)
            for b in range(2):
                dve.tensor_tensor(pa[0:64, b], pa[0:64, b], pcnt[0:64, b], ALU.mult).then_inc(windows, 1)
                dve.tensor_tensor(pa[64:P, b], pb[64:P, b], pcnt[64:P, b], ALU.mult).then_inc(windows, 1)
            for b in range(2):
                dve.wait_ge(windows, 8 + 2 * b + 2)
                dve.tensor_tensor(pa[:, b], pa[:, b], pu[:, b], ALU.subtract).then_inc(g["pool"], 1)
            for b in range(2):
                dve.wait_ge(g["pmm"], b + 1)
                dve.scalar_tensor_tensor(pg[:, b], score[:, b], pscale[:, b:b + 1], pg[:, b], ALU.mult, ALU.mult)\
                   .then_inc(g["py"], 1)
            barrier(dve, 4)

            def attention(kind):
                S, R = AT[kind], fields[kind]
                steps = attention_steps(kind)
                chunks = chunks_of(steps)
                starts = chunk_starts(chunks)
                C, N = starts[-1], len(steps)
                per = 1 if kind == "dil" else 2
                pieces = 2 if kind == "dil" else 1

                def column(x, at):
                    return x[:, at:at + 1] if isinstance(at, int) else x[:, bass.ds(at, 1)]

                def one(p, turn_, follow):
                    Q = sets[kind][turn_]

                    def rows(s):
                        i, hh, segs, width = steps[s]
                        row = R["p"][s % 2]
                        wait_pass(dve, S["tdone"], p, C, starts[s - 1] if s else starts[N - 1] - C)
                        for n, (g_, buf, c0, j0, nb, col) in enumerate(segs):
                            wait_pass(dve, S["sdone"], p, N * pieces, s * pieces + buf + 1)
                            src = score[:, 0, c0:c0 + nb * P]
                            dst = row[:, col:col + nb * P]
                            frees = kind != "dil" or n != 1
                            if kind == "dil":
                                at = sum(DIL_NB[:g_ + 1]) * P
                                ins = dve.scalar_tensor_tensor(dst, cdist[:, at - nb * P:at], column(cslope, p + 8 * g_),
                                                               src, ALU.mult, ALU.add)
                            elif kind == "fox":
                                ins = dve.scalar_tensor_tensor(dst, src, column(ccol[:, i], p * 2 + hh),
                                                               cB[turn_][hh][:, 0:width], ALU.add, ALU.subtract)
                            else:
                                ins = dve.scalar_tensor_tensor(dst, src, column(rb31, p * 2 + hh),
                                                               maskb[:, mask_offset(i):mask_offset(i + 1)], ALU.add, ALU.add)
                            ins.then_inc(S["sread"] if frees else S["pre"], 1)
                        wait_pass(dve, S["sread"], p, N * pieces, (s + 1) * pieces)
                        if kind == "fox":
                            dve.tensor_tensor(row[:, width - P:width], row[:, width - P:width], diag[:, :], ALU.add)\
                               .then_inc(S["pre"], 1)
                        elif kind == "dsa":
                            w = min(width, 2 * P)
                            near = tbias[:, p * 2 + hh, 2 * P - w:2 * P]
                            dve.tensor_tensor(row[:, width - w:width], row[:, width - w:width], near, ALU.add)\
                               .then_inc(S["pre"], 1)
                        wait_pass(dve, S["pre"], p, N, s + 1)
                        dve.tensor_reduce(R["st"][:, s:s + 1], row[:, 0:width], AX.X, ALU.max, negate=True)\
                           .then_inc(S["mx"], 1)

                    def output(s):
                        i, hh = steps[s][0:2]
                        wait_pass(dve, S["edone"], p, N, s + 1)
                        dve.reciprocal(R["st"][:, 32 + s:33 + s], R["st"][:, 16 + s:17 + s]).then_inc(S["rden"], 1)
                        wait_pass(dve, S["rden"], p, N, s + 1)
                        wait_pass(dve, S["pv"], p, C, starts[s + 1])
                        if hh == 0:
                            wait_pass(dve, S["ot"], p, NT, i - 1)
                        dh = P if kind == "dil" else 64
                        dve.tensor_scalar(R["o"][:, i % 2, hh * 64:hh * 64 + dh], obanks[s % 2][:, 0:dh],
                                          R["st"][:, 32 + s:33 + s], None, ALU.mult).then_inc(S["oev"], 1)

                    def finish(s, p=p, set_=turn_):
                        if (s + 1) % per == 0:
                            i = steps[s][0]
                            wait_pass(dve, S["ot"], p, NT, i + 1)
                            if i == 0:
                                wait_pass(dve, S["ysent"], p, 16, 0)
                            dve.scalar_tensor_tensor(R["y"][:, i * P:(i + 1) * P], obanks[s % 2][:, 256:384], 0.5,
                                                     sets[kind][set_]["g"][:, i * P:(i + 1) * P], ALU.mult, ALU.mult)\
                               .then_inc(S["y"], 1)

                    if kind == "fox":
                        wait_pass(dve, decay_in[turn_], p, 16, 32 - 16 * turn_)
                    rows(0)
                    if not (isinstance(p, int) and p == 0):
                        finish(N - 2, p - 1, 1 - turn_)
                        finish(N - 1, p - 1, 1 - turn_)
                    for t in range(N):
                        if t >= 2:
                            finish(t - 2)
                        if t + 1 < N:
                            rows(t + 1)
                        if t == 0:
                            wait_pass(dve, S["gate"], p, 2, 1)
                            dve.scalar_tensor_tensor(Q["g"], R["e"], 1.0, Q["g"], ALU.add, ALU.mult).then_inc(S["gate"], 1)
                            wait_pass(dve, S["gate"], p, 2, 2)
                        if t >= 1:
                            output(t - 1)
                    output(N - 1)
                    if not follow:
                        finish(N - 2)
                        finish(N - 1)

                passes(dve, kind, one)

            def res(c):
                return lambda half: hT[:, bass.ds(c, 1), half * 512:half * 512 + 512].rearrange("p o c -> p (o c)")

            def out_loop(base, extra):
                with dve.Fori(0, 4) as it:
                    for b in range(2):
                        for half in range(2):
                            dve.wait_ge(pass_done[half], it * 2 + (base + extra + b + 1))
                            h = res(it * 2 + b)(half)
                            dve.tensor_tensor(h, h, proj[half][:, :], ALU.add).then_inc(pass_free[half], 1)

            def ple(m, k):
                s = PL[m]
                for t in range(NT):
                    dve.wait_ge(s["h"], t + 1)
                    dve.tensor_tensor(act_lo[:, 0:2, t * P:(t + 1) * P],
                                      score[:, t % 2, 0:256].rearrange("p (b c) -> p b c", b=2),
                                      act_hi[:, 0:2, t * P:(t + 1) * P].bitcast(F32), ALU.subtract).then_inc(s["ev"], 1)
                barrier(dve, k)
                split_dve((S_PLE0, S_PLE1)[m], hT)
                dve.wait_ge(SPLIT["lo"], KB * ((S_PLE0, S_PLE1)[m] + 1))
                dve.drain().then_inc(s["r"], 8)
                base = (W_PLE0, W_PLE1)[m] + 2 + PLE_EXTRA * (m + 1)
                with dve.Fori(0, 4) as it:
                    for b in range(2):
                        for half in range(2):
                            n = it * 8 + (8 + 4 * b + 2 * half)
                            e, t = ple_e[half], ple_t[half]
                            u = upT[:, bass.ds(it * 2 + b, 1), half * 512:half * 512 + 512].rearrange("p o c -> p (o c)")
                            dve.wait_ge(pass_free[half], it * 2 + (base + b + 1))
                            dve.tensor_tensor(t, u, e, ALU.mult).then_inc(s["r"], 1)
                            dve.wait_ge(s["r"], n + 1)
                            h = res(it * 2 + b)(half)
                            dve.tensor_tensor(h, h, t, ALU.add).then_inc(s["r"], 1)
                barrier(dve, k + 1)

            attention("dsa")
            barrier(dve, 5)
            if stop > 0:
                split_dve(S_Y1, act_lo[:, :, :].bitcast(F32))
                out_loop(W_OUT1, 0)
                barrier(dve, 6)
            if stop > 1:
                norm_dve(1, False)
                barrier(dve, 7)
                norm_dve(2, True)
                barrier(dve, 8)
                dve.wait_ge(pass_free[0], W_FOXF + 1)
                dve.wait_ge(pass_free[1], W_FOXF + 1)
                dve.wait_ge(FC["x"], 16)
                dve.tensor_scalar(crow[0:16], crow[0:16], fb[0:16, 0:1], None, ALU.add).then_inc(FC["x"], 1)
                dve.wait_ge(FC["lsig"], 3)
                dve.scalar_tensor_tensor(crow[0:16], crow[0:16], 0.0, ctmp[0:16], ALU.min, ALU.subtract).then_inc(FC["lsig"], 1)
                dve.wait_ge(FC["lsig"], 4)
                dve.memset(ctmp[0:16], 1.0).then_inc(FC["lsig"], 1)
                dve.wait_ge(FC["lsig"], 5)
                dve.tensor_tensor_scan(crow[0:16], ctmp[0:16], crow[0:16], 0.0, ALU.mult, ALU.add).then_inc(FC["cum"], 1)
                dve.wait_ge(FC["t"], 1)
                dve.tensor_copy(ccol.rearrange("p t h -> p (t h)"), obank[:, 0:128]).then_inc(FC["ev"], 1)
                dve.wait_ge(FC["ev"], 1)
                attention("fox")
                barrier(dve, 9)
                split_dve(S_Y2, act_lo[:, :, :].bitcast(F32))
                out_loop(W_OUT2, 0)
                barrier(dve, 10)
                ple(0, 11)
            if stop > 2:
                norm_dve(3, True)
                barrier(dve, 13)
                dve.wait_ge(dil_in, 32)
                attention("dil")
                barrier(dve, 14)
                split_dve(S_Y3, act_lo[:, :, :].bitcast(F32))
                out_loop(W_OUT3, PLE_EXTRA)
                barrier(dve, 15)
                ple(1, 16)
                norm_dve(4, False)
                barrier(dve, 18)


_INS = ["x", "norm_g", "w_in", "gla_gate_w2", "gla_gate_b", "gla_norm_g", "rel_bias", "pool_w", "pool_scale", "w_out",
        "final_norm_g", "p_2", "fox_norm_2", "fox_w_in_2", "fox_b_f_2", "fox_w_out_2", "dil_norm_2", "dil_w_in_2",
        "dil_w_out_2", "ple_w_up_2", "ple_w_gate_2", "final_norm_2"]


def kernel(**inputs):
    import concourse.bacc as bacc
    from concourse.bass_utils import run_bass_kernel_spmd

    nc = bacc.Bacc("TRN2", target_bir_lowering=False, num_devices=1)
    arrays, a = {}, {}
    given = {name: np.ascontiguousarray(inputs[name]) for name in _INS}
    given.update(host_constants())
    for name, x in given.items():
        arrays[name + "_dram"] = x
        a[name] = nc.dram_tensor(name + "_dram", x.shape, mybir.dt.from_np(x.dtype), kind="ExternalInput").ap()
    a["out"] = nc.dram_tensor("out_dram", (1, T, D), F32, kind="ExternalOutput").ap()
    build(nc, a)
    r = run_bass_kernel_spmd(nc, [arrays], core_ids=[0])
    return r.results[0]["out_dram"]
```
